# Optimizing a Trainium2 kernel written in Bass

```python
import math
import jax, jax.numpy as jnp
from jax import lax
import numpy as np

D_MODEL = 2048
BATCH = 1
SEQ = 256
DEPTH = 1
DEC_BATCH = 8
DEC_SEQ = 1
PAST_LEN = 2048
PAGE_SIZE = 128

HEAD_DIM = 128
H_DN = 8
H_MOBA = 8
W_DN = H_DN * HEAD_DIM
W_MOBA = H_MOBA * HEAD_DIM
W_MIX = W_DN + W_MOBA
CONV_W = 4
CONV_CH = 3 * W_DN
DN_CHUNK = 64
MOBA_BLOCK = 256
MOBA_TOPK = 3
MOBA_Q_CHUNK = 16
N_BUCKETS = 32
MAX_DISTANCE = 128
N_MEM = 256
H_X = 4
W_X = H_X * HEAD_DIM
D_FF = -(-(8 * D_MODEL) // (3 * 256)) * 256
ALPHA = (2 * DEPTH) ** 0.25
BETA_INIT = (8 * DEPTH) ** -0.25
LN_EPS = 1e-5
RMS_EPS = 1e-6
L2_EPS = 1e-6

OFF_ZA = 3 * W_DN
OFF_BA = 4 * W_DN
OFF_AA = OFF_BA + H_DN
OFF_QB = OFF_AA + H_DN
OFF_KB = OFF_QB + W_MOBA
OFF_VB = OFF_KB + W_MOBA
W_IN_COLS = OFF_VB + W_MOBA

kernel_name = 'hybrid_gdn_moba_decoder_step'

def layer_norm(x, g, b):
    xf = x.astype(jnp.float32)
    mu = xf.mean(-1, keepdims=True)
    var = jnp.square(xf - mu).mean(-1, keepdims=True)
    return ((xf - mu) * lax.rsqrt(var + LN_EPS) * g.astype(jnp.float32) + b.astype(jnp.float32)).astype(x.dtype)

def post_norm(x, sub, g, b):
    return layer_norm(ALPHA * x + sub, g, b)

def l2norm(x):
    return x * lax.rsqrt(jnp.sum(x * x, -1, keepdims=True) + L2_EPS)

def short_conv(x_pad, w):
    T = x_pad.shape[1] - (CONV_W - 1)
    y = sum(w[j] * x_pad[:, j:j + T] for j in range(CONV_W))
    return jax.nn.silu(y)

def dn_prep(conv_out, ba, aa, a_log, dt_bias):
    B, T, _ = conv_out.shape
    c = conv_out.astype(jnp.float32)
    q = l2norm(c[..., :W_DN].reshape(B, T, H_DN, HEAD_DIM)) * HEAD_DIM ** -0.5
    k = l2norm(c[..., W_DN:2 * W_DN].reshape(B, T, H_DN, HEAD_DIM))
    v = c[..., 2 * W_DN:].reshape(B, T, H_DN, HEAD_DIM)
    beta = jax.nn.sigmoid(ba.astype(jnp.float32))
    g = -jnp.exp(a_log.astype(jnp.float32)) * jax.nn.softplus(
        aa.astype(jnp.float32) + dt_bias.astype(jnp.float32))
    return q, k, v, beta, g

def gated_delta_chunked(q, k, v, beta, g):
    B, T, H, D = q.shape
    C = DN_CHUNK
    NC = T // C

    def blk(x):
        return jnp.moveaxis(x.reshape((B, NC, C) + x.shape[2:]), 3, 1)

    q, k, v, beta, g = blk(q), blk(k), blk(v), blk(beta), blk(g)
    gc = jnp.cumsum(g, axis=-1)
    pos = jnp.arange(C)
    tri_incl = pos[:, None] >= pos[None, :]
    tri_strict = pos[:, None] > pos[None, :]
    decay = jnp.exp(jnp.where(tri_incl, gc[..., :, None] - gc[..., None, :], -jnp.inf))
    kbeta = k * beta[..., None]
    L = jnp.where(tri_strict, jnp.einsum('bhncd,bhned->bhnce', kbeta, k) * decay, 0.0)
    rhs = jnp.concatenate([v * beta[..., None], kbeta * jnp.exp(gc)[..., None]], -1)
    sol = lax.linalg.triangular_solve(L, rhs, left_side=True, lower=True, unit_diagonal=True)
    u0, kcum = sol[..., :D], sol[..., D:]
    qk = jnp.einsum('bhncd,bhned->bhnce', q, k) * decay
    q_dec = q * jnp.exp(gc)[..., None]
    k_dec = k * jnp.exp(gc[..., -1:] - gc)[..., None]
    g_last = jnp.exp(gc[..., -1])

    def step(S, xs):
        u0_c, kcum_c, qk_c, qd_c, kd_c, gl_c = xs
        u = u0_c - jnp.einsum('bhcd,bhde->bhce', kcum_c, S)
        o = jnp.einsum('bhcd,bhde->bhce', qd_c, S) + jnp.einsum('bhce,bhed->bhcd', qk_c, u)
        S = S * gl_c[..., None, None] + jnp.einsum('bhcd,bhce->bhde', kd_c, u)
        return S, o

    xs = (jnp.moveaxis(u0, 2, 0), jnp.moveaxis(kcum, 2, 0), jnp.moveaxis(qk, 2, 0),
          jnp.moveaxis(q_dec, 2, 0), jnp.moveaxis(k_dec, 2, 0), jnp.moveaxis(g_last, 2, 0))
    S0 = jnp.zeros((B, H, D, D), jnp.float32)
    S, o = lax.scan(step, S0, xs)
    o = jnp.transpose(o, (1, 0, 3, 2, 4)).reshape(B, T, H, D)
    return o, S

def gated_delta_recurrent(S, q, k, v, beta, g):
    def step(S, xs):
        q_t, k_t, v_t, b_t, g_t = xs
        S = S * jnp.exp(g_t)[..., None, None]
        u = b_t[..., None] * (v_t - jnp.einsum('bhde,bhd->bhe', S, k_t))
        S = S + jnp.einsum('bhd,bhe->bhde', k_t, u)
        o = jnp.einsum('bhde,bhd->bhe', S, q_t)
        return S, o

    xs = (jnp.moveaxis(q, 1, 0), jnp.moveaxis(k, 1, 0), jnp.moveaxis(v, 1, 0),
          jnp.moveaxis(beta, 1, 0), jnp.moveaxis(g, 1, 0))
    S, o = lax.scan(step, S, xs)
    return jnp.moveaxis(o, 0, 1), S

def gated_rmsnorm(o, z, w):
    B, T = o.shape[:2]
    o = o * lax.rsqrt(jnp.mean(o * o, -1, keepdims=True) + RMS_EPS) * w.astype(jnp.float32)
    return o.reshape(B, T, W_DN) * jax.nn.silu(z.astype(jnp.float32))

def t5_bucket(dist):
    d = jnp.maximum(dist, 0)
    max_exact = N_BUCKETS // 2
    ratio = jnp.log(jnp.maximum(d, max_exact).astype(jnp.float32) / max_exact) / math.log(MAX_DISTANCE / max_exact)
    large = jnp.minimum(max_exact + (ratio * (N_BUCKETS - max_exact)).astype(jnp.int32), N_BUCKETS - 1)
    return jnp.where(d < max_exact, d, large)

def moba_qkv(proj):
    B, T = proj.shape[:2]
    q = proj[..., OFF_QB:OFF_KB].reshape(B, T, H_MOBA, HEAD_DIM)
    k = proj[..., OFF_KB:OFF_VB].reshape(B, T, H_MOBA, HEAD_DIM)
    v = proj[..., OFF_VB:W_IN_COLS].reshape(B, T, H_MOBA, HEAD_DIM)
    return q, k, v

def moba_blocks(k, v):
    B, L, H, D = k.shape
    NB = -(-L // MOBA_BLOCK)
    pad = ((0, 0), (0, NB * MOBA_BLOCK - L), (0, 0), (0, 0))
    kb = jnp.pad(k, pad).reshape(B, NB, MOBA_BLOCK, H, D).transpose(0, 3, 1, 2, 4)
    vb = jnp.pad(v, pad).reshape(B, NB, MOBA_BLOCK, H, D).transpose(0, 3, 1, 2, 4)
    kmean = kb.astype(jnp.float32).mean(3)
    return kb, vb, kmean

def moba_attend(q, kb, vb, kmean, q_pos, rel_bias):
    B, Q, H, D = q.shape
    NB = kb.shape[2]
    K = min(MOBA_TOPK, NB)
    qf = q.astype(jnp.float32)
    own = q_pos // MOBA_BLOCK
    gate = jnp.einsum('bqhd,bhnd->bqhn', qf, kmean)
    past = jnp.arange(NB)[None, :] < own[:, None]
    gate = jnp.where(past[None, :, None, :], gate, -jnp.inf)
    top_s, top_i = lax.top_k(gate, K)
    sel_ok = jnp.isfinite(top_s)
    idx = jnp.concatenate([top_i, jnp.broadcast_to(own[None, :, None, None], (B, Q, H, 1))], -1)
    bi = jnp.arange(B)[:, None, None, None]
    hi = jnp.arange(H)[None, None, :, None]
    kg = kb[bi, hi, idx].astype(jnp.float32)
    vg = vb[bi, hi, idx].astype(jnp.float32)
    s = jnp.einsum('bqhd,bqhtkd->bqhtk', qf, kg) * HEAD_DIM ** -0.5
    kpos = idx[..., None] * MOBA_BLOCK + jnp.arange(MOBA_BLOCK)
    dist = q_pos[None, :, None, None, None] - kpos
    ok = jnp.concatenate([jnp.broadcast_to(sel_ok[..., None], (B, Q, H, K, MOBA_BLOCK)),
                          dist[..., K:, :] >= 0], axis=3)
    s = s + rel_bias.astype(jnp.float32)[t5_bucket(dist), jnp.arange(H)[None, None, :, None, None]]
    s = jnp.where(ok, s, -jnp.inf)
    p = jax.nn.softmax(s.reshape(B, Q, H, -1), axis=-1).reshape(s.shape)
    return jnp.einsum('bqhtk,bqhtkd->bqhd', p, vg)

def moba_prompt(q, kb, vb, kmean, rel_bias):
    B, S, H, D = q.shape
    qc = q.reshape(B, S // MOBA_Q_CHUNK, MOBA_Q_CHUNK, H, D).transpose(1, 0, 2, 3, 4)
    pos = jnp.arange(S, dtype=jnp.int32).reshape(-1, MOBA_Q_CHUNK)
    o = lax.map(lambda a: moba_attend(a[0], kb, vb, kmean, a[1], rel_bias), (qc, pos))
    return o.transpose(1, 0, 2, 3, 4).reshape(B, S, H, D)

def merge_groups(oa, ob, w_out_l, dtype):
    B, T = oa.shape[:2]
    o = jnp.concatenate([oa, ob.reshape(B, T, W_MOBA)], -1).astype(dtype)
    return o @ w_out_l

def prompt_mixer(x, w_in_l, conv_w, a_log, dt_bias, norm_w, w_out_l, rel_bias):
    proj = x @ w_in_l
    x_pad = jnp.pad(proj[..., :CONV_CH], ((0, 0), (CONV_W - 1, 0), (0, 0)))
    conv_state = x_pad[:, -(CONV_W - 1):]
    q, k, v, beta, g = dn_prep(short_conv(x_pad, conv_w), proj[..., OFF_BA:OFF_AA],
                               proj[..., OFF_AA:OFF_QB], a_log, dt_bias)
    oa, S_fin = gated_delta_chunked(q, k, v, beta, g)
    oa = gated_rmsnorm(oa, proj[..., OFF_ZA:OFF_BA], norm_w)
    qb, kb, vb = moba_qkv(proj)
    kbl, vbl, kmean = moba_blocks(kb, vb)
    ob = moba_prompt(qb, kbl, vbl, kmean, rel_bias)
    return merge_groups(oa, ob, w_out_l, x.dtype), kb, vb, S_fin, conv_state

def sample_mixer(x, k_pool, v_pool, page_table, S0, conv_state, w_in_l, conv_w, a_log, dt_bias,
                 norm_w, w_out_l, rel_bias):
    B, T, _ = x.shape
    proj = x @ w_in_l
    x_pad = jnp.concatenate([conv_state.astype(proj.dtype), proj[..., :CONV_CH]], 1)
    new_conv = x_pad[:, -(CONV_W - 1):]
    q, k, v, beta, g = dn_prep(short_conv(x_pad, conv_w), proj[..., OFF_BA:OFF_AA],
                               proj[..., OFF_AA:OFF_QB], a_log, dt_bias)
    oa, S_new = gated_delta_recurrent(S0.astype(jnp.float32), q, k, v, beta, g)
    oa = gated_rmsnorm(oa, proj[..., OFF_ZA:OFF_BA], norm_w)
    qb, kb, vb = moba_qkv(proj)
    past_k = k_pool[page_table].reshape(B, -1, H_MOBA, HEAD_DIM)
    past_v = v_pool[page_table].reshape(B, -1, H_MOBA, HEAD_DIM)
    past_len = past_k.shape[1]
    k_full = jnp.concatenate([past_k, kb.astype(past_k.dtype)], 1)
    v_full = jnp.concatenate([past_v, vb.astype(past_v.dtype)], 1)
    kbl, vbl, kmean = moba_blocks(k_full, v_full)
    q_pos = past_len + jnp.arange(T, dtype=jnp.int32)
    ob = moba_attend(qb, kbl, vbl, kmean, q_pos, rel_bias)
    return merge_groups(oa, ob, w_out_l, x.dtype), kb, vb, S_new, new_conv

def mem_kv(mem, w_kv):
    B = mem.shape[0]
    kv = mem @ w_kv
    return (kv[..., :W_X].reshape(B, N_MEM, H_X, HEAD_DIM),
            kv[..., W_X:].reshape(B, N_MEM, H_X, HEAD_DIM))

def cross_attend(h, mk, mv, w_q, w_o):
    B, T, _ = h.shape
    q = (h @ w_q).reshape(B, T, H_X, HEAD_DIM).astype(jnp.float32)
    s = jnp.einsum('bthd,bnhd->bhtn', q, mk.astype(jnp.float32)) * HEAD_DIM ** -0.5
    p = jax.nn.softmax(s, axis=-1)
    o = jnp.einsum('bhtn,bnhd->bthd', p, mv.astype(jnp.float32)).reshape(B, T, W_X).astype(h.dtype)
    return o @ w_o

def swiglu(h, w1, w2):
    gu = h @ w1
    return (jax.nn.silu(gu[..., :D_FF]) * gu[..., D_FF:]) @ w2

def setup_inputs(seed: int = 0) -> dict:
    key = jax.random.key(seed)
    ks = jax.random.split(key, 24)
    f32 = jnp.float32
    n_pages = PAST_LEN // PAGE_SIZE
    n_used = DEC_BATCH * n_pages
    n_pool = n_used + max(1, n_used // 4)

    def nrm(k, shape, scale=1.0):
        return scale * jax.random.normal(k, shape, f32)

    page_table = jax.random.permutation(ks[6], n_pool)[:n_used].reshape(DEC_BATCH, n_pages).astype(jnp.int32)
    dt = jnp.exp(jax.random.uniform(ks[10], (DEPTH, H_DN), f32, math.log(1e-3), math.log(1e-1)))
    return {
        'x_prompt': nrm(ks[0], (BATCH, SEQ, D_MODEL)),
        'x_sample': nrm(ks[1], (DEC_BATCH, DEC_SEQ, D_MODEL)),
        'cache_k': nrm(ks[2], (DEPTH, n_pool, PAGE_SIZE, H_MOBA, HEAD_DIM)),
        'cache_v': nrm(ks[3], (DEPTH, n_pool, PAGE_SIZE, H_MOBA, HEAD_DIM)),
        'cache_mem_k': nrm(ks[4], (DEPTH, DEC_BATCH, N_MEM, H_X, HEAD_DIM)),
        'cache_mem_v': nrm(ks[5], (DEPTH, DEC_BATCH, N_MEM, H_X, HEAD_DIM)),
        'state_dn': nrm(ks[7], (DEPTH, DEC_BATCH, H_DN, HEAD_DIM, HEAD_DIM), 0.1),
        'state_conv': nrm(ks[8], (DEPTH, DEC_BATCH, CONV_W - 1, CONV_CH)),
        'page_table': page_table,
        'mem_prompt': nrm(ks[9], (BATCH, N_MEM, D_MODEL)),
        'w_in': nrm(ks[11], (DEPTH, D_MODEL, W_IN_COLS), D_MODEL ** -0.5),
        'dn_conv_w': nrm(ks[12], (DEPTH, CONV_W, CONV_CH), CONV_W ** -0.5),
        'dn_a_log': jnp.log(jax.random.uniform(ks[13], (DEPTH, H_DN), f32, 1.0, 16.0)),
        'dn_dt_bias': dt + jnp.log(-jnp.expm1(-dt)),
        'dn_norm_w': 1.0 + nrm(ks[14], (DEPTH, HEAD_DIM), 0.1),
        'w_out': nrm(ks[15], (DEPTH, W_MIX, D_MODEL), W_MIX ** -0.5 * BETA_INIT),
        'rel_bias': nrm(ks[16], (N_BUCKETS, H_MOBA), 0.2),
        'x_wq': nrm(ks[17], (DEPTH, D_MODEL, W_X), D_MODEL ** -0.5),
        'x_wkv': nrm(ks[18], (DEPTH, D_MODEL, 2 * W_X), D_MODEL ** -0.5),
        'x_wo': nrm(ks[19], (DEPTH, W_X, D_MODEL), W_X ** -0.5 * BETA_INIT),
        'ffn_w1': nrm(ks[20], (DEPTH, D_MODEL, 2 * D_FF), D_MODEL ** -0.5),
        'ffn_w2': nrm(ks[21], (DEPTH, D_FF, D_MODEL), D_FF ** -0.5 * BETA_INIT),
        'ln_g': 1.0 + nrm(ks[22], (DEPTH, 3, D_MODEL), 0.05),
        'ln_b': nrm(ks[23], (DEPTH, 3, D_MODEL), 0.02),
    }

def reference(x_prompt, x_sample, cache_k, cache_v, cache_mem_k, cache_mem_v, state_dn, state_conv,
              page_table, mem_prompt, w_in, dn_conv_w, dn_a_log, dn_dt_bias, dn_norm_w, w_out, rel_bias,
              x_wq, x_wkv, x_wo, ffn_w1, ffn_w2, ln_g, ln_b):
    xp, xs = x_prompt, x_sample
    kp_l, vp_l, ks_l, vs_l, mkp_l, mvp_l, sp_l, ss_l, cp_l, cs_l = [], [], [], [], [], [], [], [], [], []
    for l in range(DEPTH):
        mix_p, kp, vp, sp, cp = prompt_mixer(xp, w_in[l], dn_conv_w[l], dn_a_log[l], dn_dt_bias[l],
                                             dn_norm_w[l], w_out[l], rel_bias)
        mix_s, k_s, v_s, s_s, c_s = sample_mixer(xs, cache_k[l], cache_v[l], page_table, state_dn[l],
                                                 state_conv[l], w_in[l], dn_conv_w[l], dn_a_log[l],
                                                 dn_dt_bias[l], dn_norm_w[l], w_out[l], rel_bias)
        xp = post_norm(xp, mix_p, ln_g[l, 0], ln_b[l, 0])
        xs = post_norm(xs, mix_s, ln_g[l, 0], ln_b[l, 0])
        mkp, mvp = mem_kv(mem_prompt, x_wkv[l])
        xp = post_norm(xp, cross_attend(xp, mkp, mvp, x_wq[l], x_wo[l]), ln_g[l, 1], ln_b[l, 1])
        xs = post_norm(xs, cross_attend(xs, cache_mem_k[l], cache_mem_v[l], x_wq[l], x_wo[l]),
                       ln_g[l, 1], ln_b[l, 1])
        xp = post_norm(xp, swiglu(xp, ffn_w1[l], ffn_w2[l]), ln_g[l, 2], ln_b[l, 2])
        xs = post_norm(xs, swiglu(xs, ffn_w1[l], ffn_w2[l]), ln_g[l, 2], ln_b[l, 2])
        kp_l.append(kp); vp_l.append(vp); ks_l.append(k_s); vs_l.append(v_s)
        mkp_l.append(mkp); mvp_l.append(mvp)
        sp_l.append(sp.astype(x_prompt.dtype)); ss_l.append(s_s.astype(state_dn.dtype))
        cp_l.append(cp); cs_l.append(c_s)
    return (xp, xs, jnp.stack(kp_l), jnp.stack(vp_l), jnp.stack(ks_l), jnp.stack(vs_l),
            jnp.stack(mkp_l), jnp.stack(mvp_l), jnp.stack(sp_l), jnp.stack(ss_l),
            jnp.stack(cp_l), jnp.stack(cs_l))


_drawn_inputs = setup_inputs


def setup_inputs(seed=0):
    import zlib

    import numpy as np

    out = dict(_drawn_inputs(seed))
    spreads = {}
    factors = {'cache_k': 2.869, 'cache_v': 2.725, 'rel_bias': 4.353, 'dn_norm_w': 2.701}
    for name, (base, spread) in spreads.items():
        noise = np.random.default_rng([zlib.crc32(name.encode()), seed]).standard_normal(out[name].shape)
        drawn = base * np.exp(spread * noise) if base else spread * noise
        out[name] = __import__('jax').numpy.asarray(drawn.astype(out[name].dtype))
    for name, factor in factors.items():
        out[name] = (out[name] * factor).astype(out[name].dtype)
    return out
```

```python
from contextlib import ExitStack
import math

import numpy as np
import concourse.bass as bass
from concourse import mybir

F32 = mybir.dt.float32
F32R = mybir.dt.float32r
I32 = mybir.dt.int32
U32 = mybir.dt.uint32
ACT = mybir.ActivationFunctionType
ALU = mybir.AluOpType
AXX = mybir.AxisListType.X
ds = bass.ds

P = 128
D_MODEL = 2048
KC = D_MODEL // P
SEQ = 256
NSAMP = 8
T = SEQ + NSAMP
H = 8
HX = 4
N_MEM = 256
PAST = 2048
PAGE = 128
PAGES = PAST // PAGE
BLOCKS = PAST // 256
TOPK = 3
D_FF = 5632
CONV_W = 4
W_IN_COLS = 7184
ALPHA = 2.0 ** 0.25
SCALE = P ** -0.5
LN_EPS, RMS_EPS, L2_EPS = 1e-5, 1e-6, 1e-6
NEG = -1e30
LEVELS = 7
CONV_ROWS = NSAMP * (CONV_W - 1) * 24
OHW = 384

_C = {}
_at = 0
for _name, _width in (("ident", P), ("flip", P), ("tri", P), ("future", P), ("ones", P), ("eye8", 64), ("eye4", 16),
                      ("levels", LEVELS * P), ("onehot_p", OHW), ("onehot_s", 130), ("own_row", 64),
                      ("iota", 8)):
    _C[_name] = (_at, _width)
    _at += _width
C_COLS = _at


def shape_constants():
    c = np.zeros((P, C_COLS), np.float32)

    def part(name):
        a, w = _C[name]
        return c[:, a:a + w]

    part("eye8")[:] = np.eye(8).reshape(1, 64)
    part("eye4")[:] = np.eye(4).reshape(1, 16)
    r = np.arange(P)
    part("ident")[:] = np.eye(P)
    part("flip")[:] = np.eye(P)[::-1]
    part("tri")[:] = r[:, None] <= r[None, :]
    part("future")[:] = np.where(r[:, None] <= r[None, :], 0.0, NEG)
    part("ones")[:] = 1.0
    for n in range(LEVELS):
        b = 1 << n
        s, t = r[:, None], r[None, :]
        part("levels")[:, n * P:(n + 1) * P] = (s // (2 * b) == t // (2 * b)) & ((t // b) % 2 == 1) & ((s // b) % 2 == 0)

    def bucket(d):
        d = np.maximum(d, 0)
        ratio = np.log(np.maximum(d, 16).astype(np.float32) / np.float32(16)) / np.float32(math.log(8))
        large = np.minimum(16 + (ratio.astype(np.float32) * np.float32(16)).astype(np.int32), 31)
        return np.where(d < 16, d, large)

    m = np.arange(OHW)
    past = m <= 255
    part("onehot_p")[bucket(255 - m[past]), m[past]] = 1.0
    part("onehot_p")[32, m[~past]] = 1.0
    s = np.concatenate([128 - np.arange(128), [129, 0]])
    part("onehot_s")[bucket(s), np.arange(130)] = 1.0
    for b in range(NSAMP):
        part("own_row")[b, b * H:(b + 1) * H] = 1.0
    part("iota")[:] = np.arange(8)[None]
    return c


class Steps:

    def __init__(self, sem, names, start=0):
        self.sem, self.start = sem, start
        self.n = len(names)
        self.order = {name: j + 1 for j, name in enumerate(names)}
        assert len(self.order) == self.n, names

    def at(self, name, i=0):
        return i * self.n + (self.start + self.order[name])

    def begin(self, i):
        return i * self.n + self.start


def wait(eng, steps, name, i=0):
    eng.wait_ge(steps.sem, steps.at(name, i))


def build(nc, a, o):
    ctx = ExitStack()
    with ctx:
        def sb(name, shape, dt=F32, stack=ctx):
            return stack.enter_context(nc.sbuf_tensor(name, shape, dt))

        def sem(name):
            return ctx.enter_context(nc.semaphore(name))

        def steps(name, names, start=0):
            return Steps(sem(name), names, start)

        x_scratch = nc.dram_tensor("x_scratch", (2, P, KC, T), F32).ap()
        gr_scratch = nc.dram_tensor("gr_scratch", (H, OHW), F32).ap()
        pid_scratch = nc.dram_tensor("pid_scratch", (64, 8), I32).ap()

        C = sb("C", [P, C_COLS])

        def const(name, rows=P):
            at, w = _C[name]
            return C[0:rows, at:at + w]

        ident, ones = const("ident"), const("ones")
        xh = sb("xh", [P, KC, T], F32R)
        xl = sb("xl", [P, KC, T], F32R)
        raw = sb("raw", [P, 2, KC, P])
        wh = sb("wh", [P, 2, KC, P], F32R)
        wl = sb("wl", [P, 2, KC, P], F32R)
        ln_gb = sb("ln_gb", [P, 2, 3, KC])
        norm_w = sb("norm_w", [P, 1])
        mem_kv = sb("mem_kv", [P, 2 * HX, N_MEM])
        mem_v = sb("mem_v", [P, 2, HX, P])
        acc = sb("acc", [P, T])

        mix = ctx.enter_context(ExitStack())
        pj = sb("pj", [P, 32, T], stack=mix)
        qb = sb("qb", [P, H, T], stack=mix)
        kv = sb("kv", [P, 2 * H, T], stack=mix)
        conv_w = sb("conv_w", [P, CONV_W, 24], stack=mix)
        sconv = sb("sconv", [P, 24, NSAMP], stack=mix)
        edge = sb("edge", [P, 24, 3 + NSAMP], stack=mix)
        gates = sb("gates", [P, 3, H], stack=mix)
        sigm = sb("sigm", [P, 3, H], stack=mix)
        beta = sb("beta", [P, H, 2], stack=mix)
        ngc = sb("ngc", [P, H, 2], stack=mix)
        bdec = sb("bdec", [P, H, 2], stack=mix)
        kdec = sb("kdec", [P, H, 2], stack=mix)
        dtot = sb("dtot", [P, H, 2], stack=mix)
        sdec = sb("sdec", [P, NSAMP, H], stack=mix)
        sbeta = sb("sbeta", [P, NSAMP, H], stack=mix)
        brow = sb("brow", [64, 130], stack=mix)
        scores = sb("scores", [P, PAGES, 64], stack=mix)

        pt = sb("pt", [P, 2 * TOPK, 64], stack=mix)
        pown = sb("pown", [P, NSAMP, H], stack=mix)
        smp = sb("smp", [P, 24, NSAMP], stack=mix)
        so = sb("so", [P, H, NSAMP], stack=mix)
        g_hc = sb("g_hc", [P, H, 2], stack=mix)
        picked = sb("picked", [64, TOPK, BLOCKS], stack=mix)

        s0 = ExitStack()
        mem_h = sb("mem_h", [P, KC, N_MEM], F32R, s0)
        mem_l = sb("mem_l", [P, KC, N_MEM], F32R, s0)
        abh = sb("abh", [P, KC, 16], F32R, s0)
        abl = sb("abl", [P, KC, 16], F32R, s0)
        s0.close()
        pj_flat = pj[:].rearrange("p a n -> p (a n)")
        stage = pj_flat[:, 0:8192].rearrange("p (s n) -> p s n", s=4)
        kv_flat = kv[:].rearrange("p a n -> p (a n)")
        rows = kv_flat[:, 0:1024].rearrange("p (s n) -> p s n", s=8)
        at = 1024

        def small(width, rows_=P):
            nonlocal at
            at += width
            return kv_flat[0:rows_, at - width:at]

        abw = small(KC * 16).rearrange("p (k n) -> p k n", k=KC)
        abt = small(T, 16)
        ab = small(48).rearrange("p (c n) -> p c n", c=3)
        a_log, dt_bias = small(8), small(8)
        y1 = small(24).rearrange("p (c n) -> p c n", c=3)
        y2 = small(24).rearrange("p (c n) -> p c n", c=3)
        y3 = small(24).rearrange("p (c n) -> p c n", c=3)
        gsp = small(64, 8).rearrange("p (b n) -> p b n", b=8)
        bsp = small(64, 8).rearrange("p (b n) -> p b n", b=8)
        relb = small(8, 33)
        relr = small(64, 32).rearrange("p (b n) -> p b n", b=8)
        gr = small(OHW, 8)
        sc = small(CONV_ROWS)
        sc_v = sc.rearrange("p (b j c) -> p j c b", b=NSAMP, j=3)
        ctmp = small(24 * NSAMP).rearrange("p (c b) -> p c b", c=24)
        assert at <= 16 * T

        sA = ExitStack()
        kring = sb("kring", [P, 4, H, P], stack=sA)
        qrow = sb("qrow", [P, H, P], stack=sA)
        qdiag = sb("qdiag", [P, H, P], stack=sA)
        srow = sb("srow", [P, PAGES, H], stack=sA)
        ct = sb("ct", [P, 3, T], stack=sA)
        cs = sb("cs", [P, 2, T], stack=sA)
        rs = sb("rs", [P, 2, T], stack=sA)
        cwi = sb("cwi", [P, CONV_W, 3], stack=sA)
        sA.close()

        sS = ExitStack()
        sraw = sb("sraw", [64, PAST], stack=sS)
        gate = sb("gate", [64, BLOCKS], stack=sS)
        best = sb("best", [64, 8], stack=sS)
        best_i = sb("best_i", [64, 8], U32, sS)
        best_f = sb("best_f", [64, 8], stack=sS)
        ptab_i = sb("ptab_i", [64, PAGES], I32, sS)
        ptab = sb("ptab", [64, PAGES], stack=sS)
        pick_page = sb("pick_page", [64, TOPK, 2, BLOCKS], stack=sS)
        page_f = sb("page_f", [64, 8], stack=sS)
        page_i = sb("page_i", [64, 8], I32, sS)
        sS.close()

        sB = ExitStack()
        def four(name, n=4):
            return sb(name, [P, n, P], stack=sB)
        tg, dec, at0, xi, yi, t1, qkd, uu = (four(n) for n in ("tg", "dec", "at0", "xi", "yi", "t1", "qkd", "uu"))
        k2, v2, q2 = (four(n) for n in ("k2", "v2", "q2"))
        cm = [four("cm0"), four("cm1")]
        egb, qd, rk, kcn, s1, sf = (four(n, 2) for n in ("egb", "qd", "rk", "kcn", "s1", "sf"))
        sB.close()

        sE = ExitStack()
        logits = sb("logits", [64, PAGES, P], stack=sE)
        probs = sb("probs", [64, TOPK * 256 + 1], stack=sE)
        pstat = sb("pstat", [64, 3], stack=sE)
        prod = sb("prod", [P, NSAMP, H], stack=sE)
        own_diag = sb("own_diag", [64, 64], stack=sE)
        kvpack = sb("kvpack", [P, 2, NSAMP, H], stack=sE)
        kvrows = sb("kvrows", [64, 2, P], stack=sE)
        epack = sb("epack", [P, 264], stack=sE)
        erows = sb("erows", [96, 3, P], stack=sE)
        memk_rows = sb("memk_rows", [P, 2, HX, P], stack=sE)
        sE.close()

        sC = ExitStack()
        att_q, att_k, att_v = (sb(n, [P, 2, SEQ], stack=sC) for n in ("att_q", "att_k", "att_v"))
        slope = sb("slope", [P, 2, SEQ], stack=sC)
        att_p = sb("att_p", [P, 2, SEQ], stack=sC)
        att_pt = sb("att_pt", [P, 3, P], stack=sC)
        vk_rows = sb("vk_rows", [P, 2, 4, P], stack=sC)
        astat = sb("astat", [P, 3, 2], stack=sC)
        state = sb("state", [P, 2, H, P], stack=sC)
        udiag = sb("udiag", [P, H, P], stack=sC)
        uk = sb("uk", [P, H, P], stack=sC)
        kq = sb("kq", [P, NSAMP, H], stack=sC)
        kqp = sb("kqp", [P, NSAMP, H], stack=sC)
        v_more = sb("v_more", [P, 2 * TOPK * P], stack=sC)
        u8 = sb("u8", [P, 6, H], stack=sC)
        sC.close()
        V_SLOT = 2 * TOPK * P
        v_slots = [pj_flat[:, 8 * T + h * V_SLOT:8 * T + (h + 1) * V_SLOT] for h in range(5)]
        v_slots += [v_more[:], scores[:].rearrange("p g n -> p (g n)")[:, 0:V_SLOT],
                    C[:, _C["levels"][0]:_C["levels"][0] + V_SLOT]]
        pm = pj_flat[:, 8 * T + 5 * V_SLOT:8 * T + 5 * V_SLOT + 384].rearrange("p (t h m) -> p t h m", t=6, h=8)
        free = _C["levels"][0] + V_SLOT
        v_rows = C[0:8, free:free + P]
        pid_row = C[0:1, free + P:free + P + 512].bitcast(I32)
        assert free + P + 512 <= C_COLS
        v_pages = [x.rearrange("p (t n) -> p t n", t=2 * TOPK) for x in v_slots]

        mix.close()
        xf = sb("xf", [P, KC, T])
        xt = sb("xt", [P, KC, T])
        mean, rstd = sb("mean", [P, T]), sb("rstd", [P, T])
        sX = ExitStack()
        xq = sb("xq", [P, HX, T], stack=sX)
        xk_rows = sb("xk_rows", [P, NSAMP, 2, HX, P], stack=sX)
        xv_rows = sb("xv_rows", [P, NSAMP, 2, HX, P], stack=sX)
        sX.close()
        spare = C[:, _C["levels"][0]:]
        at = 0

        def room(width, rows_=P):
            nonlocal at
            at += width
            return spare[0:rows_, at - width:at]

        xq_diag = room(2 * HX * P).rearrange("p (s h n) -> p s h n", s=2, h=HX)
        xs_col = room(2 * NSAMP * HX).rearrange("p (t n) -> p t n", t=2)
        xprob = room(N_MEM, NSAMP * HX)
        xp_stat = room(6 * HX).rearrange("p (s n) -> p s n", s=3)
        xs_stat = room(3, NSAMP * HX)
        xpm = mean[:, 0:256].rearrange("p (g h m) -> p g h m", g=2 * NSAMP, h=HX)
        xo_rows = xq_diag.rearrange("p s h n -> p (s h n)")[0:HX]
        assert at <= C_COLS - _C["levels"][0]
        xt_flat = xt[:].rearrange("p k n -> p (k n)")
        xatt_p, xatt_pt = xt_flat[:, 0:2048], xt_flat[:, 2048:4096]
        sF = ExitStack()
        gh = sb("gh", [P, KC, T], F32R, sF)
        gl = sb("gl", [P, KC, T], F32R, sF)
        sg = sb("sg", [P, T], stack=sF)
        gu = sb("gu", [P, 2, T], stack=sF)
        sF.close()
        y_rows = xt_flat[:, 0:4096].rearrange("p (t d) -> p t d", t=2)
        sY = ExitStack()
        ys_rows = sb("ys_rows", [NSAMP, D_MODEL], stack=sY)
        sY.close()

        psum_g = ctx.enter_context(nc.psum_tensor("psum_g", [P, 2, 512], F32))
        M = ctx.enter_context(nc.psum_tensor("M", [P, 6, 512], F32))

        d_const, d_mem, d_x, d_rows, d_small, d_ab, d_xs = (sem(n) for n in (
            "d_const", "d_mem", "d_x", "d_rows", "d_small", "d_ab", "d_xs"))
        raw_full = [sem(f"raw_full{s}") for s in range(2)]
        hi_done, raw_used, mm_done, psum_free = (sem(n) for n in ("hi_done", "raw_used", "mm_done", "psum_free"))
        gr_done = sem("gr_done")
        conv_kept = sem("conv_kept")
        s_out = sem("s_out")

        s_pe = steps("s_pe", [f"t{g}" for g in range(16)] + ["rows", "ab", "abt", "cum", "gr"])
        s_act = steps("s_act", [f"hi{g}" for g in range(16)] + [
            "xs", "abh", "cw", "ln", "sc", "sc2", "abt", "beta", "exp", "ln1", "ea", "ngc", "eg", "dtot", "kdec",
            "sdec", "sbeta", "beta2", "gr", "brow"])
        s_dve = steps("s_dve", [f"lo{g}" for g in range(16)] + [
            "xs", "abl", "ab", "y", "mn", "sp", "g", "gsp", "bsp", "tot", "bdec",
            "cv0", "cv1", "cv1a", "cv2", "cv2a"])
        s_pool = steps("s_pool", ["ab0", "neg", "relr"])

        r_pool, r_pe, r_act, r_dve = (steps(f"r_{e}", [name]) for e, name in (
            ("pool", "diag"), ("pe", "qrow"), ("act", "qrow"), ("dve", "scores")))
        a_pe = steps("a_pe", ["norm"])
        a_act = steps("a_act", ["silu_qk", "silu_v", "square", "log", "rsq"], start=1)
        a_dve = steps("a_dve", [f"w{s}" for s in range(3)] + [f"t{k}{s}" for k in (1, 2, 3) for s in range(3)] +
                      ["smp", "q", "k"])
        a_pool = steps("a_pool", ["cwi", "edge"])
        se_pe = steps("se_pe", ["rows"])
        se_act = steps("se_act", ["rows", "ghc", "ptab"])
        se_dve = steps("se_dve", ["gate", "best", "best_i", "best_f", "picked", "pick", "page_f", "page_i"])
        d_ptab, d_pid, pid_back = sem("d_ptab"), sem("d_pid"), sem("pid_back")
        lv = range(LEVELS)
        b_pe = steps("b_pe", ["gcb", "kk", "kt", "vt", "qk"] + [f"{n}{l}" for l in lv for n in ("t1_", "xt_", "yt_")
                              if (n, l) != ("xt_", LEVELS - 1)] + ["kc", "u0", "s1", "u1", "s2", "o", "rms"])
        b_act = steps("b_act", ["q2", "v2", "egb", "dec", "kcn", "u0", "s1", "u1", "sq", "oc", "log", "rsq"])
        b_dve = steps("b_dve", ["da", "qd", "at0", "qkd", "vb", "rk", "kd"] + [f"{n}{l}" for l in lv for n in (
            "t1_", "x_", "y_") if (n, l) != ("x_", LEVELS - 1)] + ["sdec", "sf", "ow", "oz"], start=1)
        b_pool = steps("b_pool", ["tg", "k2", "x", "y"] + [f"cm{l}" for l in lv])
        e_pe = steps("e_pe", ["rows", "small", "mem", "own", "pt", "pown", "kq"])
        e_act = steps("e_act", ["logits", "small", "mem", "smp", "exp", "pt"])
        e_dve = steps("e_dve", ["pack", "prod", "last"] + [f"c{n}" for n in range(BLOCKS)] +
                      ["own", "max", "rsum", "norm", "diag", "pown", "kqp", "kq"])
        e_out = sem("e_out")
        c_pe = steps("c_pe", ["sk", "tv", "sc", "ub", "pv", "tp", "vt", "oo"], start=1)
        c_act = steps("c_act", ["ks", "qs", "vs", "tv", "e0", "e1", "tp"])
        c_dve = steps("c_dve", ["pm", "kv", "vm", "u", "dg", "sd", "s1", "s2", "so", "mx", "uk", "st", "rc", "pn", "pw", "pr",
                                "pv", "oo"], start=1)
        slope_in, state_in, state_out, rows_out = ([sem(f"{n}{p}") for p in range(2)] for n in (
            "slope_in", "state_in", "state_out", "rows_out"))
        v_full = [sem(f"v_full{h}") for h in range(H)]
        v_used = sem("v_used")
        turn_stored = sem("turn_stored")
        f_pe = steps("f_pe", ["rms"])
        f_act = steps("f_act", ["sq", "log", "rsq", "hi0", "hi1"])
        f_dve = steps("f_dve", ["ow", "oz", "lo0", "lo1"])
        k_full = [sem(f"k_full{s}") for s in range(4)]
        k_used = sem("k_used")

        d_resid, x_back = sem("d_resid"), sem("x_back")
        acc_done = sem("acc_done")
        q4 = range(4)
        l_pe = steps("l_pe", ["sum", "var"])
        l_act = steps("l_act", ["mean"] + [f"s{g}" for g in q4] + ["log", "rstd"] + [f"{n}{g}" for g in q4 for n in "ah"])
        l_dve = steps("l_dve", [f"c{g}" for g in q4] + [f"n{g}" for g in q4] + [f"lo{g}" for g in q4])
        xk_full, xv_full = sem("xk_full"), sem("xv_full")
        x_pool = steps("x_pool", [f"qd{b}" for b in range(NSAMP)])
        x_pe = steps("x_pe", ["sc"] + [f"b{b}" for b in q4] + ["pt"] + [f"b{b}" for b in range(4, 8)] +
                     ["rows", "out", "dt", "do", "dr"])
        x_act = steps("x_act", ["exp", "pt", "dexp", "oh", "dor", "osh"])
        x_dve = steps("x_dve", ["mx"] + [f"t{b}" for b in range(3)] + ["rc", "pn"] + [f"t{b}" for b in range(3, 8)] +
                      ["dmx", "drc", "dpn", "xpm", "ol", "osl"])
        gh_done, gl_done = sem("gh_done"), sem("gl_done")
        y_pe = steps("y_pe", [f"g{g}" for g in range(8)] + ["s0", "s1"])
        y_act = steps("y_act", ["r0", "r1", "r2", "r3", "s0", "s1"])
        y_dve = steps("y_dve", ["r0", "r1", "r2", "r3"])
        y_ready, y_out = sem("y_ready"), sem("y_out")

        STAGES = {}
        at_unit = 0
        for name, n in (("wkv", 8), ("q", 8), ("a", 32), ("b", 16), ("out", 16), ("xq", 4), ("xo", 4),
                        ("w1a", 32), ("w2a", 16), ("w1b", 32), ("w2b", 16), ("w1c", 24), ("w2c", 16)):
            STAGES[name] = (at_unit // 4, n // 4)
            at_unit += n
        block = ctx.enter_context(nc.Block())

        def load_unit(sp, turn, u, src, nk=KC):
            sp.wait_ge(raw_used, turn * 4 + (u + 1))
            sp.dma_start(raw[:, u % 2, 0:nk], src).then_inc(raw_full[u % 2], 16)

        def upper(act, turn, u, nk=KC):
            act.wait_ge(raw_full[u % 2], turn * 32 + 16 * (u // 2 + 1))
            act.wait_ge(mm_done, turn * 4 + (u + 1))
            nc.scalar.copy(wh[:, u % 2, 0:nk], raw[:, u % 2, 0:nk]).then_inc(hi_done, 1)

        def lower(eng, turn, u, nk=KC):
            eng.wait_ge(hi_done, turn * 4 + (u + 1))
            eng.wait_ge(raw_used, turn * 4 + (u + 2))
            eng.tensor_tensor(wl[:, u % 2, 0:nk], raw[:, u % 2, 0:nk], wh[:, u % 2, 0:nk].bitcast(F32),
                                    ALU.subtract).then_inc(raw_used, 1)

        def upper_next(act, turn, u, nk=KC):
            upper(act, turn, u + 1, nk) if u < 3 else upper(act, turn + 1, 0, nk)

        def lower_next(dve, turn, u, nk=KC):
            lower(dve, turn, u + 1, nk) if u < 3 else lower(dve, turn + 1, 0, nk)

        def products(pe, out, s, w_at, x_hi, x_lo, nk, before=lambda k: None):
            for k in range(nk):
                before(k)
                hi_w, lo_w = w_at(wh, s, k), w_at(wl, s, k)
                nc.tensor.matmul(out, hi_w, x_hi(k), start=(k == 0), stop=False)
                nc.tensor.matmul(out, hi_w, x_lo(k), start=False, stop=False)
                last = nc.tensor.matmul(out, lo_w, x_hi(k), start=False, stop=(k == nk - 1))
            return last

        def unit(pe, turn, u, x_hi, x_lo, width=T, nk=KC, before=lambda k: None):
            pe.wait_ge(raw_used, turn * 4 + (u + 3))
            pe.wait_ge(psum_free, turn * 4 + (u + 1))
            products(pe, psum_g[:, u % 2, 0:width], u % 2, lambda w, s, k: w[:, s, k],
                     x_hi, x_lo, nk, before).then_inc(mm_done, 1)

        def unit_done(eng, turn, u):
            eng.wait_ge(mm_done, turn * 4 + (u + 3))

        def unit_slots(pe, turn, u, between):
            pe.wait_ge(raw_used, turn * 4 + (u + 3))
            pe.wait_ge(psum_free, turn * 4 + (u + 1))
            out = psum_g[:, u % 2, 0:T]
            for k in range(KC):
                nc.tensor.matmul(out, wh[:, u % 2, k], xh[:, k], start=(k == 0), stop=False)
                nc.tensor.matmul(out, wh[:, u % 2, k], xl[:, k], start=False, stop=False)
                last = nc.tensor.matmul(out, wl[:, u % 2, k], xh[:, k], start=False, stop=(k == KC - 1))
                if k == KC - 1:
                    last.then_inc(mm_done, 1)
                if k % 2:
                    between(8 * u + k // 2)

        def w_view(w):
            return w.rearrange("(k p) n -> p k n", p=P)

        w_in = w_view(a["w_in"][0])
        XH, XL = (lambda k: xh[:, k]), (lambda k: xl[:, k])

        def settle(eng):
            eng.wait_ge(d_const, 16)

        E_OUT = 16 * 7

        GROUPS = [("w1a", "w2a", 0, 16), ("w1b", "w2b", 16, 16), ("w1c", "w2c", 32, 12)]
        FF = D_FF // P
        END = STAGES["w2c"][0] + STAGES["w2c"][1]

        def mix_room_free(eng):
            wait(eng, f_dve, "lo1")
            eng.wait_ge(turn_stored, 8 + 2)

        SP_HEADS, POOL_HEADS, ACT_HEADS = range(0, 4), range(4, 6), range(6, 8)

        def load_values(eng, kind, i, par, heads):
            for h in heads:
                _, pages = nc.values_load_multi_w_load_instructions(
                    pid_row[:, ds((i * 16 + (par * 8 + h)) * 8, 6)], engines={kind}, min_val=0,
                    max_val=a["cache_v"].shape[1] - 1)
                eng.wait_ge(v_used, i * 16 + (par * 8 + h + 1))
                for t in range(6):
                    eng.dma_start(v_pages[h][:, t], a["cache_v"][0, ds(pages[t], 1), :, h].rearrange("a t d -> t (a d)"))\
                       .then_inc(v_full[h], 16)

        @block.sync
        def _(sp):
            sp.dma_start(C[:], a["constants"]).then_inc(d_const, 16)
            mem = a["mem_prompt"][0].rearrange("(t p) d -> p t d", p=P)
            xp = a["x_prompt"][0].rearrange("(t p) d -> p t d", p=P)
            for t in range(2):
                sp.dma_start(stage[:, t], mem[:, t]).then_inc(d_mem, 16)
            turn, n = STAGES["wkv"]
            wkv = w_view(a["x_wkv"][0])
            sp.wait_ge(raw_used, 1)
            for t in range(2):
                sp.dma_start(stage[:, 2 + t], xp[:, t]).then_inc(d_x, 16)
            with sp.Fori(0, n) as i:
                for u in range(4):
                    load_unit(sp, i, u, wkv[:, :, ds((i * 4 + u) * P, P)])
            turn, n = STAGES["q"]
            with sp.Fori(0, n) as i:
                for u in range(4):
                    load_unit(sp, i + turn, u, w_in[:, :, ds((i * 4 + u) * P + 4112, P)])
            turn, n = STAGES["a"]
            k_pages, page_table = a["cache_k"][0], a["page_table"]

            def load_pages(i, g):
                _, page = nc.values_load_multi_w_load_instructions(
                    page_table[ds(i, 1), 4 * g:4 * g + 4], engines={mybir.EngineType.SP}, min_val=0,
                    max_val=k_pages.shape[0] - 1)
                for p in range(4):
                    sp.wait_ge(k_used, i * PAGES + (4 * g + p + 1))
                    sp.dma_start(kring[:, p].rearrange("p h d -> p (h d)"),
                                 k_pages[ds(page[p], 1)].rearrange("a t h d -> t (a h d)")).then_inc(k_full[p], 16)

            load_unit(sp, turn, 0, w_in[:, :, 0:P])
            turn_b, n_b = STAGES["b"]
            with sp.Fori(0, n - 1) as i:
                for g in range(4):
                    if g < 3:
                        load_unit(sp, i + turn, g + 1, w_in[:, :, ds((i + 8 * (g + 1)) * P, P)])
                    else:
                        load_unit(sp, i + (turn + 1), 0, w_in[:, :, ds((i + 1) * P, P)])
                    load_pages(i, g)
            for g in range(4):
                if g < 3:
                    load_unit(sp, turn + n - 1, g + 1, w_in[:, :, (n - 1 + 8 * (g + 1)) * P:(n + 8 * (g + 1)) * P])
                else:
                    load_unit(sp, turn_b, 0, w_in[:, :, 5136:5136 + P])
                load_pages(n - 1, g)
            for u in range(1, 4):
                load_unit(sp, turn_b, u, w_in[:, :, 5136 + u * P:5136 + (u + 1) * P])
            with sp.Fori(1, n_b) as i:
                for u in range(4):
                    load_unit(sp, i + turn_b, u, w_in[:, :, ds((i * 4 + u) * P + 5136, P)])
            turn_out, n_out = STAGES["out"]
            w_out = w_view(a["w_out"][0])
            for u in range(2):
                load_unit(sp, turn_out, u, w_out[:, :, u * P:(u + 1) * P])
            wait(sp, b_dve, "oz", 3)
            wait(sp, e_act, "smp")
            wait(sp, e_dve, "pown")
            sp.wait_ge(e_out, E_OUT)
            sp.wait_ge(gr_done, 16)
            sp.wait_ge(d_pid, 16)
            sp.dma_start(pid_row, pid_scratch.rearrange("r (a n) -> a (r n)", a=1)).then_inc(pid_back, 16)
            sp.wait_ge(pid_back, 16)
            with sp.Fori(0, 4) as i:
                for par in range(2):
                    sp.wait_ge(turn_stored, i * 2 + (par + 1))
                    sp.dma_start(slope[:, par], bass.AP(gr_scratch.tensor, (i * 2 + par) * OHW, [[1, P], [1, SEQ]]))\
                      .then_inc(slope_in[par], 16)
                    sp.dma_start(state[:, par], a["state_dn"][0, ds(i * 2 + par, 1)].rearrange("a h d e -> d (a h) e"))\
                      .then_inc(state_in[par], 16)
                    load_values(sp, mybir.EngineType.SP, i, par, SP_HEADS)
            mix_room_free(sp)
            sp.dma_start(xf[:], x_scratch[0]).then_inc(d_resid, 16)
            sp.dma_start(xt[:], x_scratch[1]).then_inc(d_resid, 16)
            for u in (2, 3):
                load_unit(sp, turn_out, u, w_out[:, :, u * P:(u + 1) * P])
            with sp.Fori(1, n_out) as i:
                for u in range(4):
                    load_unit(sp, i + turn_out, u, w_out[:, :, ds((i * 4 + u) * P, P)])
            turn, _ = STAGES["xq"]
            x_wq = w_view(a["x_wq"][0])
            for u in range(4):
                load_unit(sp, turn, u, x_wq[:, :, u * P:(u + 1) * P])
            turn, _ = STAGES["xo"]
            x_wo = w_view(a["x_wo"][0])
            for u in range(4):
                sp.wait_ge(raw_used, turn * 4 + (u + 1))
                sp.dma_start(raw[:, u % 2].rearrange("p (k c) n -> p k (c n)", c=4), x_wo[:, :, u * 512:(u + 1) * 512])\
                  .then_inc(raw_full[u % 2], 16)
            w1, w2 = w_view(a["ffn_w1"][0]), w_view(a["ffn_w2"][0])
            for s1_, s2_, first, nk in GROUPS:
                turn, n = STAGES[s1_]
                with sp.Fori(0, n) as i:
                    for u in range(4):
                        load_unit(sp, i + turn, u, w1[:, :, ds((i * 2 + (u // 2 + first + (u % 2) * FF)) * P, P)])
                turn, n = STAGES[s2_]
                with sp.Fori(0, n) as i:
                    for u in range(4):
                        load_unit(sp, i + turn, u, w2[:, first:first + nk, ds((i * 4 + u) * P, P)], nk)
            y = o["y_prompt"][0].rearrange("(t p) d -> p t d", p=P)
            for r in range(4):
                wait(sp, y_act, f"r{r}")
                wait(sp, y_dve, f"r{r}")
                sp.dma_start(y[:, :, r * 512:(r + 1) * 512], y_rows[:, :, r * 512:(r + 1) * 512]).then_inc(y_out, 16)
            wait(sp, y_act, "s1")
            sp.dma_start(o["y_sample"][:, 0], ys_rows[:]).then_inc(y_out, 16)
            sp.wait_ge(y_out, 16 * 5)
            sp.wait_ge(conv_kept, 16)
            sp.wait_ge(s_out, 64)

        @block.gpsimd
        def _(pool):
            pool.sem_inc(turn_stored, 2)
            nc.gpsimd.memset(ab, 0.0).then_inc(s_pool.sem, 1)
            wait(pool, s_pool, "ab0")
            nc.gpsimd.memset(relb[32:33], NEG).then_inc(s_pool.sem, 1)
            pool.wait_ge(d_small, 64)
            wait(pool, s_pool, "neg")
            nc.gpsimd.tensor_copy(relr, relb[0:32].unsqueeze(1).to_broadcast([32, 8, 8])).then_inc(s_pool.sem, 1)
            wait(pool, s_dve, "lo15")
            wait(pool, s_dve, "xs")
            pool.wait_ge(psum_free, 4 * STAGES["q"][0] + 2)
            pool.dma_start(x_scratch[0], xh[:].bitcast(F32)).then_inc(d_xs, 16)
            pool.dma_start(x_scratch[1], xl[:].bitcast(F32)).then_inc(d_xs, 16)
            turn, n = STAGES["a"]
            pool.wait_ge(psum_free, 4 * turn + 2)

            def spread(i):
                nc.gpsimd.tensor_tensor(qdiag[:], ident.unsqueeze(1).to_broadcast([P, H, P]),
                                        qb[:, :, ds(i + SEQ, 1)].to_broadcast([P, H, P]),
                                        ALU.mult).then_inc(r_pool.sem, 1)

            def head_tables(i):
                wait(pool, r_pool, "diag", i)
                settle(pool)
                nc.gpsimd.tensor_copy(cwi[:], conv_w[:].rearrange("p j (s h) -> p j s h", s=3)[:, :, :, ds(i, 1)]
                                      .rearrange("p j s a -> p j (s a)")).then_inc(a_pool.sem, 1)
                pool.wait_ge(psum_free, i * 4 + (4 * turn + 5))
                settle(pool)
                nc.gpsimd.tensor_copy(edge[:].rearrange("p (s h) n -> p s h n", s=3)[:, :, ds(i, 1), :]
                                      .rearrange("p s a n -> p s (a n)"),
                                      pj[:, 0:24].rearrange("p (s h) n -> p s h n", s=3)[:, :, ds(i, 1), SEQ - 3:T]
                                      .rearrange("p s a n -> p s (a n)")).then_inc(a_pool.sem, 1)

            spread(0)
            lower(pool, turn, 1)
            lower(pool, turn, 3)
            with pool.Fori(0, n - 1) as i:
                wait(pool, r_pe, "qrow", i)
                spread(i + 1)
                head_tables(i)
                lower(pool, i + (turn + 1), 1)
                wait(pool, a_dve, "t32", i)
                lower(pool, i + (turn + 1), 3)
            head_tables(n - 1)

            wait(pool, se_dve, "page_i")
            pool.dma_start(pid_scratch, page_i[:]).then_inc(d_pid, 16)
            turn, n = STAGES["b"]

            def over(row, n=4):
                return row.unsqueeze(1).to_broadcast([P, n, P])

            wait(pool, se_act, "ghc")
            wait(pool, a_dve, "k", 7)
            pool.wait_ge(d_pid, 16)
            with pool.Fori(0, n) as i:
                nc.gpsimd.tensor_tensor(tg[:], over(const("tri")), g_hc[:, ds(i * 2, 2)].rearrange("p h c -> p (h c)")
                                        .unsqueeze(2).to_broadcast([P, 4, P]), ALU.mult).then_inc(b_pool.sem, 1)
                wait(pool, b_pool, "tg", i)
                settle(pool)
                nc.gpsimd.tensor_copy(k2[:].rearrange("p (h c) n -> p h (c n)", c=2),
                                      pj[:, ds(i * 2 + 8, 2), 0:SEQ]).then_inc(b_pool.sem, 1)
                wait(pool, b_pool, "k2", i)
                nc.gpsimd.tensor_tensor(xi[:], over(ident), over(ones), ALU.mult).then_inc(b_pool.sem, 1)
                wait(pool, b_pool, "x", i)
                nc.gpsimd.tensor_tensor(yi[:], over(ident), over(ones), ALU.mult).then_inc(b_pool.sem, 1)
                wait(pool, b_dve, "at0", i)
                for l in lv:
                    wait(pool, b_pool, f"cm{l - 1}" if l else "y", i)
                    if l >= 2:
                        wait(pool, b_pe, f"t1_{l - 2}", i)
                    mask = C[:, _C["levels"][0] + l * P:_C["levels"][0] + (l + 1) * P]
                    nc.gpsimd.tensor_tensor(cm[l % 2][:], at0[:], over(mask), ALU.mult).then_inc(b_pool.sem, 1)
                wait(pool, b_pool, f"cm{LEVELS - 1}", i)
                wait(pool, b_dve, "sf", i)
                pool.dma_start(o["dn_prompt"][0, 0, ds(i * 2, 2)].rearrange("h d e -> d h e"), sf[:]).then_inc(s_out, 16)
                wait(pool, b_dve, "oz", i)
            wait(pool, b_dve, "oz", 3)
            wait(pool, e_act, "smp")
            wait(pool, e_dve, "pown")
            pool.wait_ge(e_out, E_OUT)
            pool.wait_ge(pid_back, 16)
            with pool.Fori(0, 4) as i:
                for par in range(2):
                    load_values(pool, mybir.EngineType.Pool, i, par, POOL_HEADS)
                    wait(pool, c_act, "tv", 2 * i + par)
                    for n, name in ((0, "v_prompt"), (2, "k_prompt")):
                        pool.dma_start(o[name][0, 0, :, ds(i * 2 + par, 1)].rearrange("(t p) a d -> p t (a d)", p=P),
                                       vk_rows[:, par, n:n + 2]).then_inc(rows_out[par], 16)
                    wait(pool, c_dve, "st", 2 * i + par)
                    pool.dma_start(o["dn_sample"][0, ds(i * 2 + par, 1)].rearrange("a h d e -> d (a h) e"),
                                   state[:, par]).then_inc(state_out[par], 16)
                    pool.wait_ge(rows_out[par], i * 32 + 32)
                    pool.wait_ge(state_out[par], i * 16 + 16)
                    pool.sem_inc(turn_stored, 1)

            mix_room_free(pool)
            for b in range(NSAMP):
                for src, dst, full in ((a["cache_mem_k"], xk_rows, xk_full), (a["cache_mem_v"], xv_rows, xv_full)):
                    pool.dma_start(dst[:, b], src[0, b].rearrange("(t p) h d -> p t h d", p=P)).then_inc(full, 16)
            pool.wait_ge(psum_free, 4 * STAGES["xo"][0] + 2)
            for b in range(NSAMP):
                if b >= 2:
                    wait(pool, x_pe, f"b{b - 2}")
                nc.gpsimd.tensor_tensor(xq_diag[:, b % 2], ident.unsqueeze(1).to_broadcast([P, HX, P]),
                                        xq[:, :, SEQ + b:SEQ + b + 1].to_broadcast([P, HX, P]),
                                        ALU.mult).then_inc(x_pool.sem, 1)

        @block.scalar
        def _(act):
            act.sem_inc(psum_free, 2)
            act.sem_inc(a_act.sem, 1)
            sync = [(a["x_sample"].rearrange("b s (c p) -> (b s c) p", p=P), rows[:, 0]),
                    (a["dn_conv_w"][0].rearrange("j (c p) -> (j c) p", p=P), rows[0:96, 1]),
                    (a["ln_g"][0].rearrange("l (c p) -> (l c) p", p=P), rows[0:48, 2]),
                    (a["ln_b"][0].rearrange("l (c p) -> (l c) p", p=P), rows[48:96, 2])]
            cached = a["state_conv"][0].rearrange("b j (c p) -> (b j c) p", p=P)
            for t in range(5):
                r = min(P, CONV_ROWS - t * P)
                sync.append((cached[t * P:t * P + r], rows[0:r, 3 + t]))
            for src, dst in sync:
                act.dma_start(dst, src).then_inc(d_rows, 16)
            act.dma_start(a_log, a["dn_a_log"].to_broadcast([P, H])).then_inc(d_small, 16)
            act.dma_start(dt_bias, a["dn_dt_bias"].to_broadcast([P, H])).then_inc(d_small, 16)
            act.dma_start(relb[0:32], a["rel_bias"]).then_inc(d_small, 16)
            act.dma_start(norm_w[:], a["dn_norm_w"].rearrange("a p -> p a")).then_inc(d_small, 16)
            act.dma_start(abw, w_in[:, :, 4096:4112]).then_inc(d_ab, 16)
            for g in range(16):
                wait(act, s_pe, f"t{g}")
                dst = mem_h if g < 8 else xh
                nc.scalar.copy(dst[:, 2 * (g % 8):2 * (g % 8) + 2, 0:256],
                               M[:, g % 4].rearrange("p (c n) -> p c n", c=2)).then_inc(s_act.sem, 1)
                if g == 7:
                    upper(act, 0, 0)
            wait(act, s_pe, "rows")
            nc.scalar.copy(xh[:, :, SEQ:T], M[:, 4, 0:P].rearrange("p (b c) -> p c b", b=NSAMP)).then_inc(s_act.sem, 1)
            act.wait_ge(d_ab, 16)
            nc.scalar.copy(abh[:], abw).then_inc(s_act.sem, 1)
            nc.scalar.copy(conv_w[:].rearrange("p j c -> p (j c)"), M[:, 4, 128:224]).then_inc(s_act.sem, 1)
            nc.scalar.copy(ln_gb[:].rearrange("p g l c -> p (g l c)"), M[:, 4, 256:352]).then_inc(s_act.sem, 1)
            nc.scalar.copy(sc[:, 0:512], M[:, 5]).then_inc(s_act.sem, 1)
            nc.scalar.copy(sc[:, 512:576], M[:, 4, 384:448]).then_inc(s_act.sem, 1)
            turn, n = STAGES["wkv"]
            with act.Fori(0, n) as i:
                for u in range(4):
                    upper_next(act, i, u)
                    unit_done(act, i, u)
                    settle(act)
                    nc.scalar.copy(mem_kv[:, ds(i * 4 + u, 1)].rearrange("p a n -> p (a n)"),
                                   psum_g[:, u % 2, 0:N_MEM]).then_inc(psum_free, 1)
            wait(act, s_pe, "ab")
            nc.scalar.copy(abt, M[0:16, 0, 0:T]).then_inc(s_act.sem, 1)
            wait(act, s_dve, "ab")
            nc.scalar.activation(sigm[:], ab[:, :, 0:8], ACT.Sigmoid).then_inc(s_act.sem, 1)
            wait(act, s_dve, "mn")
            nc.scalar.activation(y2, y3, ACT.Exp).then_inc(s_act.sem, 1)
            wait(act, s_act, "exp")
            nc.scalar.activation(y2, y2, ACT.Ln, bias=1.0).then_inc(s_act.sem, 1)
            act.wait_ge(d_small, 64)
            nc.scalar.activation(a_log, a_log, ACT.Exp).then_inc(s_act.sem, 1)
            wait(act, s_pe, "cum")

            def by_head(col):
                return M[:, 2, col:col + 16].rearrange("p (h c) -> p h c", c=2)

            nc.scalar.mul(ngc[:], by_head(0), -1.0).then_inc(s_act.sem, 1)
            nc.scalar.activation(bdec[:], by_head(0), ACT.Exp).then_inc(s_act.sem, 1)
            nc.scalar.activation(dtot[:], by_head(16), ACT.Exp).then_inc(s_act.sem, 1)
            wait(act, s_dve, "tot")
            nc.scalar.activation(kdec[:], kdec[:], ACT.Exp).then_inc(s_act.sem, 1)
            nc.scalar.activation(sdec[:].rearrange("p b h -> p (b h)"), M[:, 2, 32:96], ACT.Exp).then_inc(s_act.sem, 1)
            nc.scalar.copy(sbeta[:].rearrange("p b h -> p (b h)"), M[:, 2, 96:160]).then_inc(s_act.sem, 1)
            nc.scalar.copy(beta[:], sigm[:, 0:2].rearrange("p c h -> p h c")).then_inc(s_act.sem, 1)
            wait(act, s_pe, "gr")
            nc.scalar.copy(gr, M[0:8, 3, 0:OHW]).then_inc(s_act.sem, 1)
            nc.scalar.copy(brow[:], M[0:64, 0, 0:130]).then_inc(s_act.sem, 1)
            wait(act, s_act, "gr")
            act.dma_start(gr_scratch, gr).then_inc(gr_done, 16)
            turn, n = STAGES["q"]
            with act.Fori(0, n) as i:
                for u in range(4):
                    upper_next(act, i + turn, u)
                    unit_done(act, i + turn, u)
                    settle(act)
                    nc.scalar.copy(qb[:, ds(i * 4 + u, 1)].rearrange("p a n -> p (a n)"),
                                   psum_g[:, u % 2, 0:T]).then_inc(psum_free, 1)
            turn, n = STAGES["a"]

            def queries(i):
                wait(act, r_pe, "qrow", i)
                act.wait_ge(k_used, i * PAGES + 4)
                nc.scalar.copy(qrow[:].rearrange("p (a h) n -> p a (h n)", a=2), M[:, 0:2]).then_inc(r_act.sem, 1)

            def project(i, u):
                upper_next(act, i + turn, u)
                unit_done(act, i + turn, u)
                settle(act)
                nc.scalar.activation(pj[:, ds(i + 8 * u, 1)].rearrange("p a n -> p (a n)"), psum_g[:, u % 2, 0:T],
                                     ACT.Copy if u < 3 else ACT.Silu).then_inc(psum_free, 1)

            def convolved(i):
                wait(act, a_dve, "t32", i)
                wait(act, a_dve, "smp", i)
                wait(act, a_pool, "edge", i)
                nc.scalar.activation(cs[:], ct[:, 0:2], ACT.Silu).then_inc(a_act.sem, 1)
                nc.scalar.activation(pj[:, ds(i + 16, 1)].rearrange("p a n -> p (a n)"), ct[:, 2],
                                     ACT.Silu).then_inc(a_act.sem, 1)
                wait(act, a_act, "silu_qk", i)
                nc.scalar.activation(rs[:], cs[:], ACT.Square).then_inc(a_act.sem, 1)

            def norms(i):
                wait(act, a_pe, "norm", i)
                nc.scalar.activation(rs[:], M[:, 2:4, 0:T], ACT.Ln, bias=L2_EPS).then_inc(a_act.sem, 1)
                wait(act, a_act, "log", i)
                nc.scalar.activation(rs[:], rs[:], ACT.Exp, scale=-0.5).then_inc(a_act.sem, 1)

            queries(0)
            for u in range(4):
                project(0, u)
            with act.Fori(0, n - 1) as i:
                queries(i + 1)
                project(i + 1, 0)
                convolved(i)
                project(i + 1, 1)
                norms(i)
                project(i + 1, 2)
                project(i + 1, 3)
            convolved(n - 1)
            norms(n - 1)

            for r in range(NSAMP):
                act.dma_start(ptab_i[r * H:(r + 1) * H], a["page_table"][r:r + 1].to_broadcast([H, PAGES])).then_inc(d_ptab, 16)
            wait(act, se_pe, "rows")
            nc.scalar.copy(sraw[:].rearrange("p (g n) -> p g n", g=4), M[0:64, 0:4]).then_inc(se_act.sem, 1)
            nc.scalar.copy(g_hc[:], gates[:, 0:2].rearrange("p c h -> p h c")).then_inc(se_act.sem, 1)
            act.wait_ge(d_ptab, 16 * NSAMP)
            nc.scalar.copy(ptab[:], ptab_i[:]).then_inc(se_act.sem, 1)
            turn, n = STAGES["b"]
            wait(act, a_dve, "k", 7)
            with act.Fori(0, n) as i:
                act.wait_ge(b_dve.sem, b_dve.begin(i))
                settle(act)
                nc.scalar.copy(q2[:].rearrange("p (h c) n -> p h (c n)", c=2), pj[:, ds(i * 2, 2), 0:SEQ]).then_inc(b_act.sem, 1)
                nc.scalar.copy(v2[:].rearrange("p (h c) n -> p h (c n)", c=2), pj[:, ds(i * 2 + 16, 2), 0:SEQ]).then_inc(b_act.sem, 1)

                def evacuate(u):
                    unit_done(act, i + turn, u)
                    settle(act)
                    nc.scalar.copy(kv[:, ds(i * 4 + u, 1)].rearrange("p a n -> p (a n)"),
                                   psum_g[:, u % 2, 0:T]).then_inc(psum_free, 1)

                upper_next(act, i + turn, 0)
                wait(act, b_dve, "da", i)
                nc.scalar.activation(egb[:], M[:, 0].rearrange("p (h c n) -> p h c n", h=2, c=2)[:, :, 1],
                                     ACT.Exp).then_inc(b_act.sem, 1)
                for w in range(4):
                    ins = nc.scalar.activation(dec[:, w], dec[:, w], ACT.Exp,
                                               bias=ngc[:, ds(i * 2 + w // 2, 1), w % 2:w % 2 + 1].rearrange("p a b -> p (a b)"))
                ins.then_inc(b_act.sem, 1)
                for u in range(2):
                    evacuate(u)
                    upper_next(act, i + turn, u + 1)
                wait(act, b_pe, "kc", i)
                nc.scalar.mul(kcn[:], M[:, 3, 0:256].rearrange("p (h n) -> p h n", h=2), -1.0).then_inc(b_act.sem, 1)
                wait(act, b_pe, "u0", i)
                u_v = uu[:].rearrange("p (h c) n -> p c h n", c=2)
                nc.scalar.copy(u_v[:, 0], M[:, 5, 0:256].rearrange("p (h n) -> p h n", h=2)).then_inc(b_act.sem, 1)
                wait(act, b_pe, "s1", i)
                nc.scalar.copy(s1[:], M[:, 4, 0:256].rearrange("p (h n) -> p h n", h=2)).then_inc(b_act.sem, 1)
                evacuate(2)
                upper_next(act, i + turn, 3)
                wait(act, b_pe, "u1", i)
                nc.scalar.copy(u_v[:, 1], M[:, 5, 256:512].rearrange("p (h n) -> p h n", h=2)).then_inc(b_act.sem, 1)
                wait(act, b_pe, "o", i)
                flat = lambda x: x[:].rearrange("p w n -> p (w n)")
                nc.scalar.activation(flat(at0), M[:, 1], ACT.Square).then_inc(b_act.sem, 1)
                nc.scalar.copy(flat(tg), M[:, 1]).then_inc(b_act.sem, 1)
                wait(act, b_pe, "rms", i)
                nc.scalar.activation(flat(t1), M[:, 0], ACT.Ln, bias=RMS_EPS, scale=1.0 / P).then_inc(b_act.sem, 1)
                wait(act, b_act, "log", i)
                nc.scalar.activation(flat(t1), flat(t1), ACT.Exp, scale=-0.5).then_inc(b_act.sem, 1)
                evacuate(3)
            act.wait_ge(s_out, 64)
            wait(act, b_dve, "oz", 3)
            wait(act, e_pe, "rows")
            nc.scalar.activation(logits[:, 0:12].rearrange("p (g n) t -> p g (n t)", g=3), M[0:64, 0:3], ACT.Identity,
                                 bias=brow[:, 128:129], scale=SCALE)
            nc.scalar.activation(logits[:, 12:15].rearrange("p n t -> p (n t)"), M[0:64, 3, 0:384], ACT.Identity,
                                 bias=brow[:, 128:129], scale=SCALE).then_inc(e_act.sem, 1)
            wait(act, e_pe, "small")
            nc.scalar.copy(kvrows[:].rearrange("p k n -> p (k n)"), M[0:64, 4, 0:256])
            nc.scalar.copy(erows[0:72, 0], M[0:72, 5, 0:P])
            nc.scalar.copy(erows[:, 1:3].rearrange("p k n -> p (k n)"), M[0:96, 5, P:3 * P]).then_inc(e_act.sem, 1)
            wait(act, e_pe, "mem")
            for t in range(2):
                nc.scalar.copy(memk_rows[:, t].rearrange("p h n -> p (h n)"), M[:, t])
                ins = nc.scalar.copy(mem_v[:, t].rearrange("p h n -> p (h n)"), M[:, 2 + t])
            ins.then_inc(e_act.sem, 1)
            nc.scalar.copy(smp[:], pj[:, 0:24, SEQ:T]).then_inc(e_act.sem, 1)
            wait(act, e_act, "mem")
            for name, rows_, tile in (("mem_k", (N_MEM, HX), memk_rows), ("mem_v", (N_MEM, HX), mem_v)):
                act.dma_start(o[name][0, 0].rearrange("(t p) h d -> p t h d", p=P), tile[:]).then_inc(e_out, 16)
            for n, name in enumerate(("k_sample", "v_sample")):
                act.dma_start(o[name][0, :, 0].rearrange("b h d -> (b h) d"), kvrows[:, n]).then_inc(e_out, 16)
            act.dma_start(o["conv_prompt"][0, 0].rearrange("j (c p) -> (j c) p", p=P), erows[0:72, 0]).then_inc(e_out, 16)
            for half in range(2):
                act.dma_start(o["conv_sample"][0, 4 * half:4 * half + 4, 2].rearrange("b (c p) -> b c p", p=P),
                              erows[:, 1 + half]).then_inc(e_out, 16)
            act.dma_start(o["conv_sample"][0, :, 0:2], a["state_conv"][0, :, 1:3]).then_inc(conv_kept, 16)
            wait(act, e_dve, "max")
            nc.scalar.activation(probs[:], probs[:], ACT.Exp, bias=pstat[:, 0:1], accum_out=pstat[:, 1:2]).then_inc(e_act.sem, 1)
            wait(act, e_pe, "pt")
            nc.scalar.copy(pt[:].rearrange("p j n -> p (j n)"), M[:, 0, 0:384]).then_inc(e_act.sem, 1)
            wait(act, e_dve, "pown")
            act.wait_ge(e_out, E_OUT)
            act.wait_ge(gr_done, 16)
            act.wait_ge(pid_back, 16)
            wait(act, e_pe, "pown")
            with act.Fori(0, 4) as i:
                for par in range(2):
                    j = 2 * i + par

                    def head(x):
                        return x[:, ds(j, 1), 0:SEQ].rearrange("p a n -> p (a n)")

                    act.wait_ge(c_pe.sem, c_pe.begin(j))
                    settle(act)
                    nc.scalar.copy(att_k[:, par], head(kv)).then_inc(c_act.sem, 1)
                    nc.scalar.mul(att_q[:, par], head(qb), SCALE).then_inc(c_act.sem, 1)
                    nc.scalar.copy(att_v[:, par], kv[:, ds(j + 8, 1), 0:SEQ].rearrange("p a n -> p (a n)")).then_inc(c_act.sem, 1)
                    load_values(act, mybir.EngineType.Activation, i, par, ACT_HEADS)
                    wait(act, c_pe, "tv", j)
                    act.wait_ge(turn_stored, j + 1)
                    nc.scalar.copy(vk_rows[:, par].rearrange("p w n -> p (w n)"), M[:, 3]).then_inc(c_act.sem, 1)
                    wait(act, c_dve, "mx", j)
                    nc.scalar.activation(att_p[:, 0, 0:P], M[:, 0, 0:P], ACT.Exp, bias=astat[:, 0, 0:1],
                                         accum_out=astat[:, 1, 0:1]).then_inc(c_act.sem, 1)
                    nc.scalar.activation(att_p[:, 1], M[:, 0, 256:512], ACT.Exp, bias=astat[:, 0, 1:2],
                                         accum_out=astat[:, 1, 1:2]).then_inc(c_act.sem, 1)
                    wait(act, c_pe, "tp", j)
                    nc.scalar.copy(att_pt[:].rearrange("p w n -> p (w n)"), M[:, 1, 0:384]).then_inc(c_act.sem, 1)
            wait(act, c_dve, "oo", 7)
            nc.scalar.activation(att_p[:, 0, 0:64], so[:].rearrange("p h b -> p (h b)"), ACT.Square).then_inc(f_act.sem, 1)
            wait(act, f_pe, "rms")
            nc.scalar.activation(att_p[:, 0, 64:128], M[:, 4, 0:64], ACT.Ln, bias=RMS_EPS, scale=1.0 / P).then_inc(f_act.sem, 1)
            wait(act, f_act, "log")
            nc.scalar.activation(att_p[:, 0, 64:128], att_p[:, 0, 64:128], ACT.Exp, scale=-0.5).then_inc(f_act.sem, 1)
            wait(act, f_dve, "oz")
            act.wait_ge(d_xs, 32)
            nc.scalar.copy(xh[:, 0:8], pj[:, 0:8]).then_inc(f_act.sem, 1)
            nc.scalar.copy(xh[:, 8:16], qb[:]).then_inc(f_act.sem, 1)


            def layer_norm(i):
                wait(act, l_pe, "sum", i)
                nc.scalar.mul(mean[:], M[:, 0, 0:T], 1.0 / D_MODEL).then_inc(l_act.sem, 1)
                for g in q4:
                    part = slice(4 * g, 4 * g + 4)
                    wait(act, l_dve, f"c{g}", i)
                    nc.scalar.activation(xt[:, part], xf[:, part], ACT.Square).then_inc(l_act.sem, 1)
                wait(act, l_pe, "var", i)
                nc.scalar.activation(rstd[:], M[:, 1, 0:T], ACT.Ln, bias=LN_EPS, scale=1.0 / D_MODEL).then_inc(l_act.sem, 1)
                wait(act, l_act, "log", i)
                nc.scalar.activation(rstd[:], rstd[:], ACT.Exp, scale=-0.5).then_inc(l_act.sem, 1)
                for g in q4:
                    part = slice(4 * g, 4 * g + 4)
                    wait(act, l_dve, f"n{g}", i)
                    for k in range(4 * g, 4 * g + 4):
                        ins = nc.scalar.activation(xf[:, k], xf[:, k], ACT.Identity, bias=ln_gb[:, 1, i, k:k + 1],
                                                   scale=ln_gb[:, 0, i, k:k + 1])
                    if i == 2:
                        ins.then_inc(y_ready, 1)
                        continue
                    ins.then_inc(l_act.sem, 1)
                    wait(act, l_act, f"a{g}", i)
                    nc.scalar.copy(xh[:, part], xf[:, part]).then_inc(l_act.sem, 1)

            turn, n = STAGES["out"]
            with act.Fori(0, n) as i:
                for u in range(4):
                    upper_next(act, i + turn, u)
            layer_norm(0)
            turn, n = STAGES["xq"]
            for u in range(4):
                upper_next(act, turn, u)
                unit_done(act, turn, u)
                nc.scalar.mul(xq[:, u], psum_g[:, u % 2, 0:T], SCALE).then_inc(psum_free, 1)
            wait(act, x_dve, "mx")
            for h in range(HX):
                for t in range(2):
                    w = 2 * h + t
                    ins = nc.scalar.activation(xatt_p[:, w * 256:(w + 1) * 256], M[:, h, t * 256:(t + 1) * 256], ACT.Exp,
                                               bias=xp_stat[:, 0, w:w + 1], accum_out=xp_stat[:, 1, w:w + 1])
            ins.then_inc(x_act.sem, 1)
            wait(act, x_pe, "pt")
            nc.scalar.copy(xatt_pt.rearrange("p (h n) -> p h n", h=HX), M[:, 0:4]).then_inc(x_act.sem, 1)
            wait(act, x_dve, "dmx")
            nc.scalar.activation(xprob, psum_g[0:32, 0, 0:N_MEM], ACT.Exp, bias=xs_stat[:, 0:1],
                                 accum_out=xs_stat[:, 1:2]).then_inc(x_act.sem, 1)
            wait(act, x_pe, "out")
            nc.scalar.copy(xh[:, 0:4, 0:SEQ], M[:, 4:6].rearrange("p b (h n) -> p (b h) n", h=2)).then_inc(x_act.sem, 1)
            wait(act, x_pe, "do")
            nc.scalar.copy(xo_rows.rearrange("p (g n) -> p g n", g=2), psum_g[0:4, :]).then_inc(x_act.sem, 1)
            wait(act, x_pe, "dr")
            nc.scalar.copy(xh[:, 0:4, SEQ:T], M[:, 0, 0:32].rearrange("p (b h) -> p h b", h=HX)).then_inc(x_act.sem, 1)
            turn, n = STAGES["xo"]
            for u in range(4):
                upper_next(act, turn, u)
            layer_norm(1)
            for s1_, s2_, first, nk in GROUPS:
                turn, n = STAGES[s1_]
                with act.Fori(0, n) as i:
                    for u in range(4):
                        upper_next(act, i + turn, u)
                        if u % 2 == 0:
                            unit_done(act, i + turn, u)
                            act.wait_ge(psum_free, i * 4 + (4 * turn + u + 2))
                            nc.scalar.activation(sg[:], psum_g[:, 0, 0:T], ACT.Silu).then_inc(psum_free, 1)
                turn, n = STAGES[s2_]
                last = s2_ == "w2c"
                with act.Fori(0, n - last) as i:
                    for u in range(4):
                        upper_next(act, i + turn, u, nk if last else KC)
                if last:
                    for u in range(3):
                        upper_next(act, turn + n - 1, u, nk)
            layer_norm(2)
            for r in range(4):
                wait(act, y_pe, f"g{2 * r}")
                nc.scalar.copy(y_rows[:, 0, r * 512:(r + 1) * 512], M[:, 2 + 2 * (r % 2)]).then_inc(y_act.sem, 1)
            for half in range(2):
                wait(act, y_pe, f"s{half}")
                nc.scalar.copy(ys_rows[:, half * 1024:(half + 1) * 1024].rearrange("p (b n) -> p b n", b=2),
                               (psum_g[0:8, :] if half == 0 else M[0:8, 0:2])).then_inc(y_act.sem, 1)

        @block.vector
        def _(dve):
            dve.sem_inc(raw_used, 2)
            for done in (b_dve, c_dve):
                dve.sem_inc(done.sem, 1)
            dve.sem_inc(gl_done, 2)
            dve.sem_inc(k_used, 4)
            for g in range(16):
                wait(dve, s_act, f"hi{g}")
                hi, lo = (mem_h, mem_l) if g < 8 else (xh, xl)
                part = (slice(None), slice(2 * (g % 8), 2 * (g % 8) + 2), slice(0, 256))
                nc.vector.tensor_tensor(lo[part], M[:, g % 4].rearrange("p (c n) -> p c n", c=2),
                                        hi[part].bitcast(F32), ALU.subtract).then_inc(s_dve.sem, 1)
                if g == 7:
                    lower(dve, 0, 0)
            wait(dve, s_act, "sc2")
            nc.vector.tensor_tensor(xl[:, :, SEQ:T], M[:, 4, 0:P].rearrange("p (b c) -> p c b", b=NSAMP),
                                    xh[:, :, SEQ:T].bitcast(F32), ALU.subtract).then_inc(s_dve.sem, 1)
            wait(dve, s_act, "abh")
            nc.vector.tensor_tensor(abl[:], abw, abh[:].bitcast(F32), ALU.subtract).then_inc(s_dve.sem, 1)
            turn, n = STAGES["wkv"]
            with dve.Fori(0, n) as i:
                for u in range(4):
                    lower_next(dve, i, u)
            wait(dve, s_pe, "abt")
            wait(dve, s_pool, "ab0")
            nc.vector.tensor_copy(ab[:, 0:2], M[:, 1, 0:32].rearrange("p (c n) -> p c n", c=2))
            nc.vector.tensor_copy(ab[0:8, 2], M[0:8, 1, 32:48]).then_inc(s_dve.sem, 1)
            wait(dve, s_dve, "ab")
            dve.wait_ge(d_small, 64)

            def by_chunk(row):
                return row.unsqueeze(1).to_broadcast([P, 3, H])

            nc.vector.tensor_tensor(y1, ab[:, :, 8:16], by_chunk(dt_bias), ALU.add).then_inc(s_dve.sem, 1)
            wait(dve, s_dve, "y")
            nc.vector.scalar_tensor_tensor(y3, y1, -1.0, y1, ALU.mult, ALU.min).then_inc(s_dve.sem, 1)
            wait(dve, s_act, "ea")
            nc.vector.scalar_tensor_tensor(y3, y1, 0.0, y2, ALU.max, ALU.add).then_inc(s_dve.sem, 1)
            wait(dve, s_dve, "sp")
            nc.vector.scalar_tensor_tensor(gates[:], y3, -1.0, by_chunk(a_log), ALU.mult, ALU.mult).then_inc(s_dve.sem, 1)
            wait(dve, s_dve, "g")
            own = const("own_row", 8).rearrange("p (b h) -> p b h", b=8)
            nc.vector.tensor_tensor(gsp, own, gates[0:8, 2].unsqueeze(1).to_broadcast([8, 8, 8]),
                                    ALU.mult).then_inc(s_dve.sem, 1)
            nc.vector.tensor_tensor(bsp, own, sigm[0:8, 2].unsqueeze(1).to_broadcast([8, 8, 8]),
                                    ALU.mult).then_inc(s_dve.sem, 1)
            wait(dve, s_act, "dtot")
            nc.vector.tensor_tensor(kdec[:], M[:, 2, 16:32].rearrange("p (h c) -> p h c", c=2), ngc[:],
                                    ALU.add).then_inc(s_dve.sem, 1)
            wait(dve, s_act, "beta2")
            nc.vector.tensor_tensor(bdec[:], bdec[:], beta[:], ALU.mult).then_inc(s_dve.sem, 1)
            for j in range(3):
                w = conv_w[:, j].unsqueeze(2).to_broadcast([P, 24, NSAMP])
                if j:
                    wait(dve, s_dve, "cv0" if j == 1 else "cv1a")
                nc.vector.tensor_tensor(ctmp if j else sconv[:], sc_v[:, j], w, ALU.mult).then_inc(s_dve.sem, 1)
                if j:
                    wait(dve, s_dve, f"cv{j}")
                    nc.vector.tensor_tensor(sconv[:], sconv[:], ctmp, ALU.add).then_inc(s_dve.sem, 1)
            turn, n = STAGES["q"]
            with dve.Fori(0, n) as i:
                for u in range(4):
                    lower_next(dve, i + turn, u)
            turn, n = STAGES["a"]
            head = lambda s, i: pj[:, ds(i + 8 * s, 1)].rearrange("p a n -> p (a n)")

            def score(i, pages_):
                for p in pages_:
                    dve.wait_ge(k_full[p % 4], i * 64 + 16 * (p // 4 + 1))
                    for h in range(H):
                        last = nc.vector.tensor_tensor_reduce(
                            out=kring[:, p % 4, h], in0=kring[:, p % 4, h], in1=qrow[:, h], scale=1.0,
                            scalar=0.0, op0=ALU.mult, op1=ALU.add, accum_out=srow[:, p, h:h + 1])
                    last.then_inc(k_used, 1)

            def keep_scores(i):
                dve.wait_ge(k_used, i * PAGES + (PAGES + 4))
                nc.vector.tensor_copy(scores[:, :, ds(i * H, H)], srow[:]).then_inc(r_dve.sem, 1)

            def convolve(i):
                wait(dve, a_pool, "cwi", i)
                dve.wait_ge(psum_free, i * 4 + (4 * turn + 5))
                for s in range(3):
                    nc.vector.tensor_scalar(ct[:, s], head(s, i), cwi[:, 3, s:s + 1], None, ALU.mult).then_inc(a_dve.sem, 1)
                for k in (1, 2, 3):
                    for s in range(3):
                        wait(dve, a_dve, f"t{k - 1}{s}" if k > 1 else f"w{s}", i)
                        nc.vector.scalar_tensor_tensor(ct[:, s, k:SEQ], head(s, i)[:, 0:SEQ - k], cwi[:, 3 - k, s:s + 1],
                                                       ct[:, s, k:SEQ], ALU.mult, ALU.add).then_inc(a_dve.sem, 1)
                nc.vector.tensor_tensor(ct[:, :, SEQ:T], ct[:, :, SEQ:T],
                                        sconv[:].rearrange("p (s h) b -> p s h b", s=3)[:, :, ds(i, 1), :]
                                        .rearrange("p s a b -> p s (a b)"), ALU.add).then_inc(a_dve.sem, 1)

            def normalise(i):
                wait(dve, a_act, "rsq", i)
                nc.vector.scalar_tensor_tensor(head(0, i), cs[:, 0], SCALE, rs[:, 0], ALU.mult, ALU.mult).then_inc(a_dve.sem, 1)
                nc.vector.tensor_tensor(head(1, i), cs[:, 1], rs[:, 1], ALU.mult).then_inc(a_dve.sem, 1)

            wait(dve, r_act, "qrow", 0)
            for u in range(4):
                if u % 2:
                    lower_next(dve, turn, u)
                score(0, range(4 * u, 4 * u + 4))
            keep_scores(0)
            with dve.Fori(0, n - 1) as i:
                convolve(i)
                wait(dve, r_act, "qrow", i + 1)
                wait(dve, r_dve, "scores", i)
                score(i + 1, range(0, 4))
                lower_next(dve, i + (turn + 1), 1)
                score(i + 1, range(4, 8))
                normalise(i)
                score(i + 1, range(8, 12))
                lower_next(dve, i + (turn + 1), 3)
                score(i + 1, range(12, 16))
                keep_scores(i + 1)
            convolve(n - 1)
            normalise(n - 1)

            wait(dve, se_act, "rows")
            nc.vector.tensor_reduce(gate[:], sraw[:].rearrange("p (n t) -> p n t", n=BLOCKS), AXX, ALU.add).then_inc(se_dve.sem, 1)
            wait(dve, se_dve, "gate")
            nc.vector.max(best[:], gate[:]).then_inc(se_dve.sem, 1)
            wait(dve, se_dve, "best")
            nc.vector.max_index(best_i[:], best[:], gate[:]).then_inc(se_dve.sem, 1)
            wait(dve, se_dve, "best_i")
            nc.vector.tensor_copy(best_f[:], best_i[:]).then_inc(se_dve.sem, 1)
            wait(dve, se_dve, "best_f")
            nc.vector.tensor_tensor(picked[:], best_f[:, 0:TOPK].unsqueeze(2).to_broadcast([64, TOPK, BLOCKS]),
                                    const("iota", 64).unsqueeze(1).to_broadcast([64, TOPK, BLOCKS]),
                                    ALU.is_equal).then_inc(se_dve.sem, 1)
            wait(dve, se_dve, "picked")
            wait(dve, se_act, "ptab")
            for half in range(2):
                last = nc.vector.tensor_tensor(
                    pick_page[:, :, half], picked[:],
                    ptab[:].rearrange("p (n s) -> p s n", s=2)[:, half:half + 1].to_broadcast([64, TOPK, BLOCKS]), ALU.mult)
            last.then_inc(se_dve.sem, 1)
            wait(dve, se_dve, "pick")
            nc.vector.tensor_reduce(page_f[:, 0:6], pick_page[:].rearrange("p j s n -> p (j s) n"), AXX,
                                    ALU.add).then_inc(se_dve.sem, 1)
            wait(dve, se_dve, "page_f")
            nc.vector.memset(page_i[:, 6:8], 0)
            nc.vector.tensor_copy(page_i[:, 0:6], page_f[:, 0:6]).then_inc(se_dve.sem, 1)
            turn, n = STAGES["b"]

            def bank(b, n=4):
                return M[:, b, 0:n * P].rearrange("p (w n) -> p w n", n=P)

            def over(row, n=4):
                return row.unsqueeze(1).to_broadcast([P, n, P])

            with dve.Fori(0, n) as i:
                def by_w(table):
                    return table[:, ds(i * 2, 2)].rearrange("p h c -> p (h c)").unsqueeze(2).to_broadcast([P, 4, P])

                def second(table):
                    return table[:, ds(i * 2, 2), 1:2].to_broadcast([P, 2, P])

                def odd(x):
                    return x.rearrange("p (h c) n -> p h c n", c=2)[:, :, 1]

                def vec(ins):
                    ins.then_inc(b_dve.sem, 1)

                wait(dve, b_pe, "gcb", i)
                nc.vector.tensor_tensor(dec[:], bank(0), over(const("future")), ALU.add).then_inc(b_dve.sem, 1)
                wait(dve, b_act, "egb", i)
                nc.vector.tensor_tensor(qd[:], odd(q2[:]), egb[:], ALU.mult).then_inc(b_dve.sem, 1)
                wait(dve, b_act, "dec", i)
                wait(dve, b_pe, "kk", i)
                nc.vector.tensor_tensor(at0[:], bank(1), dec[:], ALU.mult).then_inc(b_dve.sem, 1)
                lower_next(dve, i + turn, 0)
                wait(dve, b_pe, "qk", i)
                nc.vector.tensor_tensor(qkd[:], bank(4), dec[:], ALU.mult).then_inc(b_dve.sem, 1)
                nc.vector.tensor_tensor(v2[:], bank(3), by_w(beta), ALU.mult).then_inc(b_dve.sem, 1)
                nc.vector.tensor_tensor(rk[:], odd(bank(2)), second(bdec), ALU.mult).then_inc(b_dve.sem, 1)
                nc.vector.tensor_tensor(k2[:], bank(2), by_w(kdec), ALU.mult).then_inc(b_dve.sem, 1)
                for l in lv:
                    wait(dve, b_pe, f"t1_{l}", i)
                    nc.vector.tensor_tensor(t1[:], bank(0), by_w(beta), ALU.mult).then_inc(b_dve.sem, 1)
                    if l < LEVELS - 1:
                        wait(dve, b_pe, f"xt_{l}", i)
                        if l:
                            wait(dve, b_dve, f"x_{l - 1}", i)
                        nc.vector.tensor_tensor(xi[:], xi[:], bank(1), ALU.subtract).then_inc(b_dve.sem, 1)
                    wait(dve, b_pe, f"yt_{l}", i)
                    if l:
                        wait(dve, b_dve, f"y_{l - 1}", i)
                    nc.vector.tensor_tensor(yi[:], yi[:], bank(2), ALU.subtract).then_inc(b_dve.sem, 1)
                    if l in (1, 5):
                        lower_next(dve, i + turn, 1 if l == 1 else 2)
                wait(dve, b_act, "s1", i)
                nc.vector.tensor_tensor(sf[:], s1[:], second(dtot), ALU.mult).then_inc(b_dve.sem, 1)
                wait(dve, b_pe, "s2", i)
                wait(dve, b_dve, "sdec", i)
                nc.vector.tensor_tensor(sf[:], sf[:], M[:, 4, 256:512].rearrange("p (h n) -> p h n", h=2),
                                        ALU.add).then_inc(b_dve.sem, 1)
                lower_next(dve, i + turn, 3)
                wait(dve, b_act, "rsq", i)
                nc.vector.scalar_tensor_tensor(tg[:], tg[:], norm_w[:, 0:1], t1[:], ALU.mult, ALU.mult).then_inc(b_dve.sem, 1)
                wait(dve, b_dve, "ow", i)
                nc.vector.tensor_tensor(pj[:, ds(i * 2, 2), 0:SEQ], tg[:].rearrange("p (h c) n -> p h (c n)", c=2),
                                        pj[:, ds(i * 2 + 24, 2), 0:SEQ], ALU.mult).then_inc(b_dve.sem, 1)
                dve.wait_ge(s_out, i * 16 + 16)
            dve.wait_ge(b_dve.sem, b_dve.begin(4))
            dve.wait_ge(s_out, 64)
            dve.wait_ge(psum_free, 4 * (turn + n) + 2)
            for k in range(2):
                nc.vector.tensor_copy(kvpack[:, k].rearrange("p b h -> p h b"), kv[:, 8 * k:8 * k + 8, SEQ:T])
            nc.vector.tensor_copy(epack[:, 0:72].rearrange("p (j c) -> p c j", j=3), edge[:, :, 0:3])
            nc.vector.tensor_copy(epack[:, 72:264].rearrange("p (b c) -> p c b", b=8), edge[:, :, 3:11]).then_inc(e_dve.sem, 1)
            nc.vector.tensor_tensor(prod[:].rearrange("p b h -> p h b"), qb[:, :, SEQ:T], kv[:, 0:8, SEQ:T],
                                    ALU.mult).then_inc(e_dve.sem, 1)
            wait(dve, e_act, "logits")
            nc.vector.scalar_tensor_tensor(logits[:, 15], M[0:64, 3, 384:512], SCALE, brow[:, 0:P], ALU.mult,
                                           ALU.add).then_inc(e_dve.sem, 1)
            wait(dve, e_dve, "last")
            for n_ in range(BLOCKS):
                block_n = logits[:, 2 * n_:2 * n_ + 2].rearrange("p s t -> p (s t)")
                if n_:
                    wait(dve, e_dve, f"c{n_ - 1}")
                for j in range(TOPK):
                    dst = probs[:, 256 * j:256 * (j + 1)]
                    if n_ == 0:
                        ins = nc.vector.tensor_scalar(dst, block_n, picked[:, j, 0:1], None, ALU.mult)
                    else:
                        ins = nc.vector.scalar_tensor_tensor(dst, block_n, picked[:, j, n_:n_ + 1], dst, ALU.mult, ALU.add)
                ins.then_inc(e_dve.sem, 1)
            wait(dve, e_pe, "own")
            nc.vector.scalar_tensor_tensor(probs[:, 768:769], M[0:64, 4, 0:1], SCALE, brow[:, 129:130], ALU.mult,
                                           ALU.add).then_inc(e_dve.sem, 1)
            wait(dve, e_dve, "own")
            nc.vector.tensor_reduce(pstat[:, 0:1], probs[:], AXX, ALU.max, negate=True).then_inc(e_dve.sem, 1)
            wait(dve, e_act, "exp")
            nc.vector.reciprocal(pstat[:, 2:3], pstat[:, 1:2]).then_inc(e_dve.sem, 1)
            wait(dve, e_dve, "rsum")
            nc.vector.tensor_scalar(probs[:], probs[:], pstat[:, 2:3], None, ALU.mult).then_inc(e_dve.sem, 1)
            wait(dve, e_dve, "norm")
            nc.vector.tensor_scalar(own_diag[:], ident[0:64, 0:64], probs[:, 768:769], None, ALU.mult).then_inc(e_dve.sem, 1)
            wait(dve, e_pe, "pown")
            nc.vector.tensor_copy(pown[:].rearrange("p b h -> p (b h)"), M[:, 1, 0:64]).then_inc(e_dve.sem, 1)
            dve.wait_ge(e_out, E_OUT)
            wait(dve, e_act, "pt")
            nc.vector.tensor_tensor(kqp[:], smp[:, 0:8].rearrange("p h b -> p b h"), smp[:, 8:16].rearrange("p h b -> p b h"),
                                    ALU.mult).then_inc(e_dve.sem, 1)
            wait(dve, e_pe, "kq")
            nc.vector.tensor_copy(kq[:].rearrange("p b h -> p (b h)"), M[:, 2, 0:64]).then_inc(e_dve.sem, 1)
            with dve.Fori(0, 4) as i:
                for par in range(2):
                    j = 2 * i + par

                    def samp(at):
                        return smp[:, at:at + 8, ds(j, 1)].rearrange("p h a -> p (h a)")

                    def table(x):
                        return x[:, ds(j, 1)].rearrange("p a h -> p (a h)")

                    def wide(col):
                        return col.unsqueeze(2).to_broadcast([P, H, P])

                    dve.wait_ge(c_dve.sem, c_dve.begin(j))
                    nc.vector.tensor_tensor(pm, pt[:, :, ds(j * 8, 8)].unsqueeze(3).to_broadcast([P, 6, 8, 8]),
                                            const("eye8").rearrange("p (h m) -> p h m", h=8).unsqueeze(1)
                                            .to_broadcast([P, 6, 8, 8]), ALU.mult).then_inc(c_dve.sem, 1)
                    wait(dve, c_pe, "sk", j)
                    s_qk = psum_g[:, 0, 0:16].rearrange("p (h a) -> p a h", a=2)
                    nc.vector.tensor_tensor(u8[:, 0], s_qk[:, 1], table(sdec), ALU.mult).then_inc(c_dve.sem, 1)
                    wait(dve, c_dve, "kv", j)
                    nc.vector.tensor_tensor(u8[:, 1], samp(16), u8[:, 0], ALU.subtract).then_inc(c_dve.sem, 1)
                    wait(dve, c_dve, "vm", j)
                    nc.vector.tensor_tensor(u8[:, 2], u8[:, 1], table(sbeta), ALU.mult).then_inc(c_dve.sem, 1)
                    wait(dve, c_dve, "u", j)
                    nc.vector.tensor_tensor(udiag[:], ident.unsqueeze(1).to_broadcast([P, H, P]), wide(u8[:, 2]),
                                            ALU.mult).then_inc(c_dve.sem, 1)
                    nc.vector.tensor_tensor(state[:, par], state[:, par], wide(table(sdec)), ALU.mult).then_inc(c_dve.sem, 1)
                    nc.vector.tensor_tensor(u8[:, 4], s_qk[:, 0], table(sdec), ALU.mult).then_inc(c_dve.sem, 1)
                    nc.vector.tensor_tensor(u8[:, 5], u8[:, 2], table(kq[:]), ALU.mult).then_inc(c_dve.sem, 1)
                    wait(dve, c_dve, "s2", j)
                    nc.vector.tensor_tensor(so[:, :, ds(j, 1)].rearrange("p h a -> p (h a)"), u8[:, 4], u8[:, 5],
                                            ALU.add).then_inc(c_dve.sem, 1)
                    wait(dve, c_pe, "sc", j)
                    nc.vector.tensor_reduce(astat[:, 0, 0:1], M[:, 0, 0:P], AXX, ALU.max, negate=True)
                    nc.vector.tensor_reduce(astat[:, 0, 1:2], M[:, 0, 256:512], AXX, ALU.max, negate=True).then_inc(c_dve.sem, 1)
                    wait(dve, c_pe, "ub", j)
                    nc.vector.tensor_tensor(uk[:], M[:, 4:6].rearrange("p a (h n) -> p (a h) n", n=P), wide(samp(8)),
                                            ALU.mult).then_inc(c_dve.sem, 1)
                    wait(dve, c_dve, "uk", j)
                    nc.vector.tensor_tensor(state[:, par], state[:, par], uk[:], ALU.add).then_inc(c_dve.sem, 1)
                    wait(dve, c_act, "e1", j)
                    nc.vector.reciprocal(astat[:, 2], astat[:, 1]).then_inc(c_dve.sem, 1)
                    wait(dve, c_dve, "rc", j)
                    nc.vector.tensor_scalar(att_p[:, 0, 0:P], att_p[:, 0, 0:P], astat[:, 2, 0:1], None, ALU.mult)
                    nc.vector.tensor_scalar(att_p[:, 1], att_p[:, 1], astat[:, 2, 1:2], None, ALU.mult).then_inc(c_dve.sem, 1)
                    nc.vector.tensor_tensor(u8[:, 3], kv[:, 8:16, ds(j + SEQ, 1)].rearrange("p h a -> p (h a)"), table(pown),
                                            ALU.mult).then_inc(c_dve.sem, 1)
                    wait(dve, c_pe, "pv", j)
                    nc.vector.tensor_copy(v_rows, psum_g[0:8, 1, 0:P]).then_inc(c_dve.sem, 1)
                    wait(dve, c_pe, "vt", j)
                    wait(dve, c_dve, "pw", j)
                    nc.vector.tensor_tensor(qb[:, :, ds(j + SEQ, 1)].rearrange("p h a -> p (h a)"), psum_g[:, 1, P:P + 8],
                                            u8[:, 3], ALU.add).then_inc(c_dve.sem, 1)
                    wait(dve, c_pe, "oo", j)
                    nc.vector.tensor_scalar(qb[:, ds(j, 1), 0:SEQ].rearrange("p a n -> p (a n)"), M[:, 2, 0:SEQ], 1.0, None,
                                            ALU.mult).then_inc(c_dve.sem, 1)
            wait(dve, f_act, "rsq")
            nc.vector.scalar_tensor_tensor(so[:].rearrange("p h b -> p (h b)"), so[:].rearrange("p h b -> p (h b)"),
                                           norm_w[:, 0:1], att_p[:, 0, 64:128], ALU.mult, ALU.mult).then_inc(f_dve.sem, 1)
            wait(dve, f_dve, "ow")
            nc.vector.tensor_tensor(pj[:, 0:8, SEQ:T], so[:], pj[:, 24:32, SEQ:T], ALU.mult).then_inc(f_dve.sem, 1)
            for n_, src in ((0, pj), (1, qb)):
                wait(dve, f_act, f"hi{n_}")
                nc.vector.tensor_tensor(xl[:, 8 * n_:8 * n_ + 8], src[:, 0:8], xh[:, 8 * n_:8 * n_ + 8].bitcast(F32),
                                        ALU.subtract).then_inc(f_dve.sem, 1)


            def add_to_acc(i, m, src):
                dve.wait_ge(acc_done, m + (17 * i + 1))
                nc.vector.tensor_tensor(acc[:], acc[:], src, ALU.add).then_inc(acc_done, 1)

            def clear_acc(i):
                if i:
                    wait(dve, l_act, "mean", i - 1)
                nc.vector.memset(acc[:], 0.0).then_inc(acc_done, 1)

            def layer_norm(i):
                wait(dve, l_act, "mean", i)
                for g in q4:
                    part = xf[:, 4 * g:4 * g + 4]
                    nc.vector.tensor_tensor(part, part, mean[:].unsqueeze(1).to_broadcast([P, 4, T]),
                                            ALU.subtract).then_inc(l_dve.sem, 1)
                wait(dve, l_act, "rstd", i)
                for g in q4:
                    part = xf[:, 4 * g:4 * g + 4]
                    nc.vector.tensor_tensor(part, part, rstd[:].unsqueeze(1).to_broadcast([P, 4, T]),
                                            ALU.mult).then_inc(l_dve.sem, 1)
                for g in q4:
                    if i < 2:
                        wait(dve, l_act, f"h{g}", i)
                        part = slice(4 * g, 4 * g + 4)
                        nc.vector.tensor_tensor(xl[:, part], xf[:, part], xh[:, part].bitcast(F32),
                                                ALU.subtract).then_inc(l_dve.sem, 1)

            clear_acc(0)
            dve.wait_ge(d_resid, 32)
            nc.vector.tensor_tensor(xf[:], xf[:], xt[:], ALU.add).then_inc(x_back, 1)
            dve.wait_ge(x_back, 1)
            turn, n = STAGES["out"]
            with dve.Fori(0, n) as i:
                for u in range(4):
                    lower_next(dve, i + turn, u)
                    unit_done(dve, i + turn, u)
                    m = xf[:, ds(i * 4 + u, 1)].rearrange("p a n -> p (a n)")
                    nc.vector.scalar_tensor_tensor(m, m, ALPHA, psum_g[:, u % 2, 0:T], ALU.mult, ALU.add).then_inc(psum_free, 1)
                    dve.wait_ge(psum_free, i * 4 + (4 * turn + u + 3))
                    add_to_acc(0, i * 4 + u, m)
            layer_norm(0)
            turn, n = STAGES["xq"]
            for u in range(4):
                lower_next(dve, turn, u)
            wait(dve, x_pe, "sc")
            nc.vector.tensor_reduce(xp_stat[:, 0], M[:, 0:4].rearrange("p h (t n) -> p (h t) n", t=2), AXX, ALU.max,
                                    negate=True).then_inc(x_dve.sem, 1)
            dve.wait_ge(xk_full, 16 * NSAMP)

            def score(b):
                wait(dve, x_pe, f"b{b}")
                for t in range(2):
                    for h in range(HX):
                        last = nc.vector.tensor_tensor_reduce(
                            out=xk_rows[:, b, t, h], in0=xk_rows[:, b, t, h], in1=M[:, 4 + b % 2, h * P:(h + 1) * P],
                            scale=1.0, scalar=0.0, op0=ALU.mult, op1=ALU.add, accum_out=xs_col[:, t, 4 * b + h:4 * b + h + 1])
                last.then_inc(x_dve.sem, 1)

            for b in range(3):
                score(b)
            wait(dve, x_act, "exp")
            nc.vector.reciprocal(xp_stat[:, 2], xp_stat[:, 1]).then_inc(x_dve.sem, 1)
            wait(dve, x_dve, "rc")
            att = xatt_p.rearrange("p (w n) -> p w n", w=8)
            nc.vector.tensor_tensor(att, att, xp_stat[:, 2].unsqueeze(2).to_broadcast([P, 8, 256]),
                                    ALU.mult).then_inc(x_dve.sem, 1)
            for b in range(3, NSAMP):
                score(b)
            wait(dve, x_pe, "rows")
            nc.vector.tensor_reduce(xs_stat[:, 0:1], psum_g[0:32, 0, 0:N_MEM], AXX, ALU.max, negate=True).then_inc(x_dve.sem, 1)
            wait(dve, x_act, "dexp")
            nc.vector.reciprocal(xs_stat[:, 2:3], xs_stat[:, 1:2]).then_inc(x_dve.sem, 1)
            wait(dve, x_dve, "drc")
            nc.vector.tensor_scalar(xprob, xprob, xs_stat[:, 2:3], None, ALU.mult).then_inc(x_dve.sem, 1)
            wait(dve, x_pe, "dt")
            nc.vector.tensor_tensor(xpm, psum_g[:, 1, 0:64].rearrange("p (g h) -> p g h", h=HX).unsqueeze(3)
                                    .to_broadcast([P, 2 * NSAMP, HX, HX]),
                                    const("eye4").rearrange("p (h m) -> p h m", h=HX).unsqueeze(1)
                                    .to_broadcast([P, 2 * NSAMP, HX, HX]), ALU.mult).then_inc(x_dve.sem, 1)
            wait(dve, x_act, "oh")
            nc.vector.tensor_tensor(xl[:, 0:4, 0:SEQ], M[:, 4:6].rearrange("p b (h n) -> p (b h) n", h=2),
                                    xh[:, 0:4, 0:SEQ].bitcast(F32), ALU.subtract).then_inc(x_dve.sem, 1)
            wait(dve, x_act, "osh")
            nc.vector.tensor_tensor(xl[:, 0:4, SEQ:T], M[:, 0, 0:32].rearrange("p (b h) -> p h b", h=HX),
                                    xh[:, 0:4, SEQ:T].bitcast(F32), ALU.subtract).then_inc(x_dve.sem, 1)
            clear_acc(1)
            turn, n = STAGES["xo"]
            for u in range(4):
                lower_next(dve, turn, u)
                unit_done(dve, turn, u)
                for at_, banks in (((4 * u, M[:, 0:4, 0:T]),) if u % 2 == 0 else
                                   ((4 * u, M[:, 4:6, 0:T]), (4 * u + 2, psum_g[:, :, 0:T]))):
                    dst = xf[:, at_:at_ + banks.shape[1]]
                    last = nc.vector.scalar_tensor_tensor(dst, dst, ALPHA, banks, ALU.mult, ALU.add)
                last.then_inc(psum_free, 1)
                dve.wait_ge(psum_free, 4 * turn + (u + 3))
                for c in range(4):
                    add_to_acc(1, 4 * u + c, xf[:, 4 * u + c])
            layer_norm(1)
            for s1_, s2_, first, nk in GROUPS:
                turn, n = STAGES[s1_]
                with dve.Fori(0, n) as i:
                    for u in range(4):
                        lower_next(dve, i + turn, u)
                        if u % 2:
                            half = u // 2
                            j = i * 2 + half
                            unit_done(dve, i + turn, u)
                            dve.wait_ge(psum_free, i * 4 + (4 * turn + u + 2))
                            dve.wait_ge(gl_done, j + (first + 1))
                            nc.vector.tensor_tensor(gu[:, half], sg[:], psum_g[:, 1, 0:T], ALU.mult).then_inc(psum_free, 1)
                            dve.wait_ge(psum_free, i * 4 + (4 * turn + u + 3))
                            nc.vector.tensor_scalar(gh[:, ds(j, 1)].rearrange("p a n -> p (a n)"), gu[:, half], 1.0, None,
                                                    ALU.mult).then_inc(gh_done, 1)
                            dve.wait_ge(gh_done, j + (first + 1))
                            nc.vector.tensor_tensor(gl[:, ds(j, 1)].rearrange("p a n -> p (a n)"), gu[:, half],
                                                    gh[:, ds(j, 1)].bitcast(F32).rearrange("p a n -> p (a n)"),
                                                    ALU.subtract).then_inc(gl_done, 1)
                turn, n = STAGES[s2_]
                last = s2_ == "w2c"
                if last:
                    clear_acc(2)

                def onto_residual(i, u, m, nk_next):
                    if nk_next:
                        lower_next(dve, i + turn, u, nk_next)
                    unit_done(dve, i + turn, u)
                    nc.vector.scalar_tensor_tensor(m, m, ALPHA if s2_ == "w2a" else 1.0, psum_g[:, u % 2, 0:T], ALU.mult,
                                                   ALU.add).then_inc(psum_free, 1)

                with dve.Fori(0, n - last) as i:
                    for u in range(4):
                        m = xf[:, ds(i * 4 + u, 1)].rearrange("p a n -> p (a n)")
                        onto_residual(i, u, m, nk if last else KC)
                        if last:
                            dve.wait_ge(psum_free, i * 4 + (4 * turn + u + 3))
                            add_to_acc(2, i * 4 + u, m)
                if last:
                    for u in range(4):
                        m = xf[:, 4 * (n - 1) + u]
                        onto_residual(n - 1, u, m, nk if u < 3 else 0)
                        dve.wait_ge(psum_free, (n - 1) * 4 + (4 * turn + u + 3))
                        add_to_acc(2, 4 * (n - 1) + u, m)
            layer_norm(2)
            for r in range(4):
                wait(dve, y_pe, f"g{2 * r + 1}")
                nc.vector.tensor_copy(y_rows[:, 1, r * 512:(r + 1) * 512], M[:, 3 + 2 * (r % 2)]).then_inc(y_dve.sem, 1)

        @block.tensor
        def _(pe):
            pe.sem_inc(mm_done, 2)
            pe.sem_inc(c_pe.sem, 1)
            pe.wait_ge(d_const, 16)
            for g in range(16):
                if g % 8 == 0:
                    pe.wait_ge(d_mem if g == 0 else d_x, 32)
                if g >= 4:
                    wait(pe, s_dve, f"lo{g - 4}")
                for c in range(2):
                    for t in range(2):
                        last = nc.tensor.transpose(M[:, g % 4, (2 * c + t) * P:(2 * c + t + 1) * P],
                                                   stage[:, 2 * (g // 8) + t, (2 * (g % 8) + c) * P:(2 * (g % 8) + c + 1) * P],
                                                   ident)
                last.then_inc(s_pe.sem, 1)
            pe.wait_ge(d_rows, 9 * 16)
            for r, n, src in ((4, P, 0), (4, 96, 1), (4, 96, 2), (4, 64, 7), (5, P, 3), (5, P, 4), (5, P, 5), (5, P, 6)):
                col = {0: 0, 1: 128, 2: 256, 7: 384, 3: 0, 4: 128, 5: 256, 6: 384}[src]
                last = nc.tensor.transpose(M[:, r, col:col + n], rows[0:n, src], ident[0:n, 0:n])
            last.then_inc(s_pe.sem, 1)
            turn, n = STAGES["wkv"]
            with pe.Fori(0, n) as i:
                for u in range(4):
                    unit(pe, i, u, lambda k: mem_h[:, k], lambda k: mem_l[:, k], width=N_MEM)
            wait(pe, s_dve, "abl")
            products(pe, M[0:16, 0, 0:T], 0, lambda w, s, k: (abh if w is wh else abl)[:, k], XH, XL,
                     KC).then_inc(s_pe.sem, 1)
            wait(pe, s_act, "abt")
            nc.tensor.transpose(M[:, 1, 0:16], abt[:, 0:P], ident[0:16, 0:16])
            nc.tensor.transpose(M[:, 1, 16:32], abt[:, P:2 * P], ident[0:16, 0:16])
            nc.tensor.transpose(M[0:8, 1, 32:48], abt[:, SEQ:T], ident[0:16, 0:16]).then_inc(s_pe.sem, 1)
            wait(pe, s_dve, "bsp")
            g_hc = gates[:, 0:2].rearrange("p c h -> p h c")
            nc.tensor.matmul(M[:, 2, 0:16], const("tri"), g_hc, start=True, stop=True)
            nc.tensor.matmul(M[:, 2, 16:32], ones, g_hc, start=True, stop=True)
            nc.tensor.matmul(M[:, 2, 32:96], const("ones", 8), gsp.rearrange("p b h -> p (b h)"), start=True, stop=True)
            nc.tensor.matmul(M[:, 2, 96:160], const("ones", 8), bsp.rearrange("p b h -> p (b h)"), start=True,
                             stop=True).then_inc(s_pe.sem, 1)
            wait(pe, s_pool, "relr")
            nc.tensor.matmul(M[0:8, 3, 0:OHW], relb, const("onehot_p", 33), start=True, stop=True)
            nc.tensor.matmul(M[0:64, 0, 0:130], relr.rearrange("p b h -> p (b h)"), const("onehot_s", 32), start=True,
                             stop=True).then_inc(s_pe.sem, 1)
            turn, n = STAGES["q"]
            with pe.Fori(0, n) as i:
                for u in range(4):
                    unit(pe, i + turn, u, XH, XL)
            turn, n = STAGES["a"]

            def spread(i):
                wait(pe, r_pool, "diag", i)
                for half in range(2):
                    last = nc.tensor.matmul(M[:, half], ones, qdiag[:, 4 * half:4 * half + 4].rearrange("p h n -> p (h n)"),
                                            start=True, stop=True)
                last.then_inc(r_pe.sem, 1)

            def norms(i):
                wait(pe, a_act, "square", i)
                for s in range(2):
                    last = nc.tensor.matmul(M[:, 2 + s, 0:T], ones, rs[:, s], start=True, stop=True)
                last.then_inc(a_pe.sem, 1)

            spread(0)
            for u in range(4):
                unit(pe, turn, u, XH, XL)
            with pe.Fori(0, n - 1) as i:
                wait(pe, r_act, "qrow", i)
                spread(i + 1)
                unit(pe, i + (turn + 1), 0, XH, XL)
                unit(pe, i + (turn + 1), 1, XH, XL)
                norms(i)
                unit(pe, i + (turn + 1), 2, XH, XL)
                unit(pe, i + (turn + 1), 3, XH, XL)
            norms(n - 1)
            wait(pe, r_dve, "scores", 7)
            pe.wait_ge(a_act.sem, a_act.begin(8))
            for page in range(PAGES):
                last = nc.tensor.transpose(M[0:64, page // 4, (page % 4) * P:(page % 4 + 1) * P], scores[:, page], ident)
            last.then_inc(se_pe.sem, 1)
            turn, n = STAGES["b"]
            wait(pe, se_act, "rows")
            with pe.Fori(0, n) as i:
                def each(out, lhs, rhs, ws=range(4)):
                    for w in ws:
                        last = nc.tensor.matmul(out(w), lhs(w), rhs(w), start=True, stop=True)
                    last.then_inc(b_pe.sem, 1)

                def col(bank, w, at=0):
                    return M[:, bank, at + w * P:at + (w + 1) * P]

                def delta(slot):
                    if slot == 0:
                        wait(pe, b_pool, "tg", i)
                        nc.tensor.matmul(M[:, 0], ones, tg[:].rearrange("p w n -> p (w n)"), start=True,
                                         stop=True).then_inc(b_pe.sem, 1)
                    elif slot == 1:
                        wait(pe, b_pool, "k2", i)
                        each(lambda w: col(1, w), lambda w: k2[:, w], lambda w: k2[:, w])
                    elif slot == 2:
                        for w in range(4):
                            last = nc.tensor.transpose(col(2, w), k2[:, w], ident)
                        last.then_inc(b_pe.sem, 1)
                        wait(pe, b_act, "v2", i)
                        for w in range(4):
                            last = nc.tensor.transpose(col(3, w), v2[:, w], ident)
                        last.then_inc(b_pe.sem, 1)
                    elif slot == 3:
                        each(lambda w: col(4, w), lambda w: k2[:, w], lambda w: q2[:, w])
                    elif slot < 5 + 2 * LEVELS and slot >= 5:
                        l, second = divmod(slot - 5, 2)
                        if not second:
                            wait(pe, b_pool, f"cm{l}", i)
                            if l:
                                wait(pe, b_dve, f"x_{l - 1}", i)
                            each(lambda w: col(0, w), lambda w: cm[l % 2][:, w], lambda w: xi[:, w])
                        else:
                            wait(pe, b_dve, f"t1_{l}", i)
                            if l:
                                wait(pe, b_dve, f"y_{l - 1}", i)
                            else:
                                wait(pe, b_dve, "kd", i)
                            if l < LEVELS - 1:
                                each(lambda w: col(1, w), lambda w: yi[:, w], lambda w: t1[:, w])
                            each(lambda w: col(2, w), lambda w: t1[:, w], lambda w: yi[:, w])
                    elif slot == 5 + 2 * LEVELS:
                        wait(pe, b_dve, f"y_{LEVELS - 1}", i)
                        each(lambda h: col(3, h), lambda h: rk[:, h], lambda h: yi[:, 2 * h + 1], range(2))
                        each(lambda h: col(5, h), lambda h: yi[:, 2 * h], lambda h: v2[:, 2 * h], range(2))
                    elif slot == 7 + 2 * LEVELS:
                        wait(pe, b_act, "u0", i)
                        each(lambda h: col(4, h), lambda h: k2[:, 2 * h], lambda h: uu[:, 2 * h], range(2))
                    elif slot == 9 + 2 * LEVELS:
                        wait(pe, b_act, "s1", i)
                        for h in range(2):
                            nc.tensor.matmul(col(5, h, 256), yi[:, 2 * h + 1], v2[:, 2 * h + 1], start=True, stop=False)
                            last = nc.tensor.matmul(col(5, h, 256), kcn[:, h], s1[:, h], start=False, stop=True)
                        last.then_inc(b_pe.sem, 1)
                    elif slot == 11 + 2 * LEVELS:
                        wait(pe, b_act, "u1", i)
                        each(lambda h: col(4, h, 256), lambda h: k2[:, 2 * h + 1], lambda h: uu[:, 2 * h + 1], range(2))
                        for h in range(2):
                            nc.tensor.matmul(col(1, 2 * h), uu[:, 2 * h], qkd[:, 2 * h], start=True, stop=True)
                            nc.tensor.matmul(col(1, 2 * h + 1), uu[:, 2 * h + 1], qkd[:, 2 * h + 1], start=True, stop=False)
                            last = nc.tensor.matmul(col(1, 2 * h + 1), s1[:, h], qd[:, h], start=False, stop=True)
                        last.then_inc(b_pe.sem, 1)
                    elif slot == 13 + 2 * LEVELS:
                        wait(pe, b_act, "sq", i)
                        nc.tensor.matmul(M[:, 0], ones, at0[:].rearrange("p w n -> p (w n)"), start=True,
                                         stop=True).then_inc(b_pe.sem, 1)

                for u in range(4):
                    unit_slots(pe, i + turn, u, delta)
            wait(pe, b_dve, "oz", 3)
            wait(pe, b_act, "rsq", 3)
            for page in range(PAGES):
                last = nc.tensor.transpose(M[0:64, page // 4, (page % 4) * P:(page % 4 + 1) * P], scores[:, page], ident)
            last.then_inc(e_pe.sem, 1)
            wait(pe, e_dve, "pack")
            for k in range(2):
                nc.tensor.transpose(M[0:64, 4, k * P:(k + 1) * P], kvpack[:, k].rearrange("p b h -> p (b h)"), ident)
            nc.tensor.transpose(M[0:72, 5, 0:P], epack[:, 0:72], ident)
            nc.tensor.transpose(M[0:96, 5, P:2 * P], epack[:, 72:168], ident)
            nc.tensor.transpose(M[0:96, 5, 2 * P:3 * P], epack[:, 168:264], ident).then_inc(e_pe.sem, 1)
            wait(pe, e_act, "logits")
            wait(pe, e_dve, "last")
            for t in range(2):
                for h in range(HX):
                    nc.tensor.transpose(M[:, t, h * P:(h + 1) * P], mem_kv[:, h, t * P:(t + 1) * P], ident)
                    last = nc.tensor.transpose(M[:, 2 + t, h * P:(h + 1) * P], mem_kv[:, HX + h, t * P:(t + 1) * P], ident)
            last.then_inc(e_pe.sem, 1)
            wait(pe, e_dve, "prod")
            wait(pe, e_act, "small")
            nc.tensor.matmul(M[0:64, 4, 0:1], prod[:].rearrange("p b h -> p (b h)"), ones[:, 0:1], start=True,
                             stop=True).then_inc(e_pe.sem, 1)
            wait(pe, e_dve, "norm")
            for t in range(6):
                last = nc.tensor.transpose(M[:, 0, t * 64:(t + 1) * 64], probs[:, t * P:(t + 1) * P], ident[0:64, 0:64])
            last.then_inc(e_pe.sem, 1)
            wait(pe, e_dve, "diag")
            nc.tensor.matmul(M[:, 1, 0:64], const("ones", 64), own_diag[:], start=True, stop=True).then_inc(e_pe.sem, 1)
            wait(pe, e_act, "pt")
            wait(pe, e_dve, "pown")
            wait(pe, e_dve, "kqp")
            nc.tensor.matmul(M[:, 2, 0:64], ones, kqp[:].rearrange("p b h -> p (b h)"), start=True, stop=True).then_inc(e_pe.sem, 1)
            wait(pe, e_dve, "kq")
            pe.sem_inc(v_used, H)
            with pe.Fori(0, 4) as i:
                for par in range(2):
                    j = 2 * i + par
                    pe.wait_ge(state_in[par], i * 16 + 16)
                    pe.wait_ge(c_dve.sem, c_dve.begin(j))
                    for h in range(H):
                        last = nc.tensor.matmul(psum_g[:, 0, 2 * h:2 * h + 2], state[:, par, h],
                                                smp[:, h:h + 9:8, ds(j, 1)].rearrange("p a b -> p (a b)"),
                                                start=True, stop=True)
                    last.then_inc(c_pe.sem, 1)
                    wait(pe, c_act, "vs", j)
                    for n_, src in ((0, att_v), (1, att_k)):
                        for t in range(2):
                            last = nc.tensor.transpose(M[:, 3, (2 * n_ + t) * P:(2 * n_ + t + 1) * P],
                                                       src[:, par, t * P:(t + 1) * P], ident)
                    last.then_inc(c_pe.sem, 1)
                    pe.wait_ge(slope_in[par], i * 16 + 16)
                    for t in range(2):
                        out = M[:, 0, 256 * t:256 * t + P * (t + 1)]
                        nc.tensor.matmul(out, att_q[:, par, t * P:(t + 1) * P], att_k[:, par, 0:P * (t + 1)],
                                         start=True, stop=False)
                        last = nc.tensor.matmul(out, const("flip"), slope[:, par, P * (1 - t):SEQ], start=False, stop=True)
                    last.then_inc(c_pe.sem, 1)
                    wait(pe, c_dve, "dg", j)
                    for half in range(2):
                        last = nc.tensor.matmul(M[:, 4 + half], ones,
                                                udiag[:, 4 * half:4 * half + 4].rearrange("p h n -> p (h n)"),
                                                start=True, stop=True)
                    last.then_inc(c_pe.sem, 1)
                    wait(pe, c_dve, "pm", j)
                    for h in range(H):
                        pe.wait_ge(v_full[h], i * (2 * 96) + 96 * (par + 1))
                        for t in range(6):
                            last = nc.tensor.matmul(psum_g[0:8, 1, 0:P], pm[:, t, h], v_pages[h][:, t],
                                                    start=(h == 0 and t == 0), stop=(h == H - 1 and t == 5))
                        last.then_inc(v_used, 1)
                    pe.drain().then_inc(c_pe.sem, 1)
                    wait(pe, c_dve, "pr", j)
                    for w, (q, k) in enumerate(((0, 0), (1, 0), (1, 1))):
                        last = nc.tensor.transpose(M[:, 1, w * P:(w + 1) * P], att_p[:, q, k * P:(k + 1) * P], ident)
                    last.then_inc(c_pe.sem, 1)
                    nc.tensor.transpose(psum_g[:, 1, P:P + 8], v_rows, ident[0:8, 0:8]).then_inc(c_pe.sem, 1)
                    wait(pe, c_act, "tp", j)
                    nc.tensor.matmul(M[:, 2, 0:P], vk_rows[:, par, 0], att_pt[:, 0], start=True, stop=True)
                    nc.tensor.matmul(M[:, 2, P:SEQ], vk_rows[:, par, 0], att_pt[:, 1], start=True, stop=False)
                    nc.tensor.matmul(M[:, 2, P:SEQ], vk_rows[:, par, 1], att_pt[:, 2], start=False,
                                     stop=True).then_inc(c_pe.sem, 1)
            wait(pe, f_act, "sq")
            nc.tensor.matmul(M[:, 4, 0:64], ones, att_p[:, 0, 0:64], start=True, stop=True).then_inc(f_pe.sem, 1)


            def layer_norm(i):
                pe.wait_ge(acc_done, 17 * (i + 1))
                nc.tensor.matmul(M[:, 0, 0:T], ones, acc[:], start=True, stop=True).then_inc(l_pe.sem, 1)
                for g in q4:
                    wait(pe, l_act, f"s{g}", i)
                    for k in range(4 * g, 4 * g + 4):
                        last = nc.tensor.matmul(M[:, 1, 0:T], ones, xt[:, k], start=(k == 0), stop=(k == KC - 1))
                last.then_inc(l_pe.sem, 1)

            def normed(i):
                return lambda k: wait(pe, l_dve, f"lo{k // 4}", i) if k % 4 == 0 else None

            wait(pe, f_dve, "lo1")
            turn, n = STAGES["out"]
            with pe.Fori(0, n) as i:
                for u in range(4):
                    unit(pe, i + turn, u, XH, XL)
            layer_norm(0)
            turn, n = STAGES["xq"]
            for u in range(4):
                unit(pe, turn, u, XH, XL, before=normed(0) if u == 0 else lambda k: None)
            pe.wait_ge(psum_free, 4 * (turn + n) + 2)
            wait(pe, l_act, "rstd", 0)
            for h in range(HX):
                for t in range(2):
                    last = nc.tensor.matmul(M[:, h, t * 256:(t + 1) * 256], xq[:, h, t * P:(t + 1) * P], mem_kv[:, h],
                                            start=True, stop=True)
            last.then_inc(x_pe.sem, 1)

            def spread(b):
                wait(pe, x_pool, f"qd{b}")
                if b >= 2:
                    wait(pe, x_dve, f"t{b - 2}")
                nc.tensor.matmul(M[:, 4 + b % 2], ones, xq_diag[:, b % 2].rearrange("p h n -> p (h n)"), start=True,
                                 stop=True).then_inc(x_pe.sem, 1)

            for b in range(4):
                spread(b)
            wait(pe, x_dve, "pn")
            for h in range(HX):
                for q in range(2):
                    for t in range(2):
                        last = nc.tensor.transpose(M[:, h, t * 256 + q * P:t * 256 + (q + 1) * P],
                                                   xatt_p[:, (2 * h + q) * 256 + t * P:(2 * h + q) * 256 + (t + 1) * P], ident)
            last.then_inc(x_pe.sem, 1)
            for b in range(4, NSAMP):
                spread(b)
            wait(pe, x_dve, "t7")
            for t in range(2):
                last = nc.tensor.transpose(psum_g[0:32, 0, t * P:(t + 1) * P], xs_col[:, t], ident)
            last.then_inc(x_pe.sem, 1)
            wait(pe, x_act, "pt")
            for h in range(HX):
                for t in range(2):
                    last = nc.tensor.matmul(M[:, 4 + h // 2, (h % 2) * 256:(h % 2 + 1) * 256], mem_v[:, t, h],
                                            xatt_pt[:, h * 512 + t * 256:h * 512 + (t + 1) * 256], start=(t == 0), stop=(t == 1))
            last.then_inc(x_pe.sem, 1)
            wait(pe, x_dve, "dpn")
            for t in range(2):
                last = nc.tensor.transpose(psum_g[:, 1, 32 * t:32 * (t + 1)], xprob[:, t * P:(t + 1) * P], ident[0:32, 0:32])
            last.then_inc(x_pe.sem, 1)
            wait(pe, x_dve, "xpm")
            pe.wait_ge(xv_full, 16 * NSAMP)
            for b in range(NSAMP):
                for h in range(HX):
                    for t in range(2):
                        last = nc.tensor.matmul(psum_g[0:4, b // 4, (b % 4) * P:(b % 4 + 1) * P], xpm[:, t * NSAMP + b, h],
                                                xv_rows[:, b, t, h], start=(h == 0 and t == 0), stop=(h == HX - 1 and t == 1))
            last.then_inc(x_pe.sem, 1)
            wait(pe, x_act, "dor")
            for b in range(NSAMP):
                last = nc.tensor.transpose(M[:, 0, HX * b:HX * (b + 1)], xo_rows[:, b * P:(b + 1) * P], ident[0:HX, 0:HX])
            last.then_inc(x_pe.sem, 1)
            wait(pe, x_dve, "osl")
            turn, n = STAGES["xo"]
            for u in range(4):
                pe.wait_ge(raw_used, turn * 4 + (u + 3))
                pe.wait_ge(psum_free, turn * 4 + (u + 1))
                for c in range(4):
                    bank_ = M[:, c, 0:T] if u % 2 == 0 else M[:, 4 + c, 0:T] if c < 2 else psum_g[:, c - 2, 0:T]
                    last = products(pe, bank_, u % 2, lambda w, s_, k: w[:, s_, 4 * k + c], XH, XL, 4)
                last.then_inc(mm_done, 1)
            layer_norm(1)
            turn, n = STAGES["w1a"]
            for u in range(4):
                unit(pe, turn, u, XH, XL, before=normed(1) if u == 0 else lambda k: None)
            for s1_, s2_, first, nk in GROUPS:
                turn, n = STAGES[s1_]
                with pe.Fori(1 if s1_ == "w1a" else 0, n) as i:
                    for u in range(4):
                        unit(pe, i + turn, u, XH, XL)
                pe.wait_ge(gl_done, first + nk + 2)
                turn, n = STAGES[s2_]
                with pe.Fori(0, n) as i:
                    for u in range(4):
                        unit(pe, i + turn, u, lambda k: gh[:, k], lambda k: gl[:, k], nk=nk)
            layer_norm(2)
            for r in range(4):
                pe.wait_ge(y_ready, r + 1)
                for t in range(2):
                    if r >= 2:
                        wait(pe, (y_act, y_dve)[t], f"r{r - 2}")
                    for c in range(4):
                        last = nc.tensor.transpose(M[:, 2 + 2 * (r % 2) + t, c * P:(c + 1) * P],
                                                   xf[:, 4 * r + c, t * P:(t + 1) * P], ident)
                    last.then_inc(y_pe.sem, 1)
            for half in range(2):
                for c in range(8):
                    bank_ = (psum_g if half == 0 else M)[0:8, c // 4, (c % 4) * P:(c % 4 + 1) * P]
                    last = nc.tensor.transpose(bank_, xf[:, 8 * half + c, SEQ:T], ident)
                last.then_inc(y_pe.sem, 1)


_IN = ["x_prompt", "x_sample", "cache_k", "cache_v", "cache_mem_k", "cache_mem_v", "state_dn", "state_conv",
       "page_table", "mem_prompt", "w_in", "dn_conv_w", "dn_a_log", "dn_dt_bias", "dn_norm_w", "w_out", "rel_bias",
       "x_wq", "x_wkv", "x_wo", "ffn_w1", "ffn_w2", "ln_g", "ln_b"]
_OUT = [("y_prompt", (1, SEQ, D_MODEL)), ("y_sample", (NSAMP, 1, D_MODEL)),
        ("k_prompt", (1, 1, SEQ, H, P)), ("v_prompt", (1, 1, SEQ, H, P)),
        ("k_sample", (1, NSAMP, 1, H, P)), ("v_sample", (1, NSAMP, 1, H, P)),
        ("mem_k", (1, 1, N_MEM, HX, P)), ("mem_v", (1, 1, N_MEM, HX, P)),
        ("dn_prompt", (1, 1, H, P, P)), ("dn_sample", (1, NSAMP, H, P, P)),
        ("conv_prompt", (1, 1, CONV_W - 1, 24 * P)), ("conv_sample", (1, NSAMP, CONV_W - 1, 24 * P))]


def kernel(**inputs):
    import concourse.bacc as bacc
    from concourse.bass_utils import run_bass_kernel_spmd as run

    nc = bacc.Bacc("TRN2", target_bir_lowering=False, num_devices=1)
    arrays, a = {}, {}
    for name in _IN:
        arrays[name] = np.ascontiguousarray(inputs[name])
    arrays["constants"] = shape_constants()
    for name, x in arrays.items():
        a[name] = nc.dram_tensor(name, x.shape, mybir.dt.from_np(x.dtype), kind="ExternalInput").ap()
    o = {name: nc.dram_tensor("out_" + name, shape, F32, kind="ExternalOutput").ap() for name, shape in _OUT}
    build(nc, a, o)
    r = run(nc, [arrays], core_ids=[0])
    return tuple(r.results[0]["out_" + name] for name, _ in _OUT)
```
